# Optimizing a Trainium2 kernel written in Bass

```python
import jax, jax.numpy as jnp
from jax import lax
import numpy as np

D_MODEL = 1024
BATCH = 1
SEQ = 256
DEPTH = 2

GRID_W = 64
CTX_LEN = 256
N_MIXERS = 2
N_MOD = 9
D_FF = 2816
GMLP_D_FF = 6 * D_MODEL
GMLP_HALF = GMLP_D_FF // 2
CHUNK = 128
GMLP_GROUPS = 8
HEAD_DIM = 128
N_HEADS = D_MODEL // HEAD_DIM
N_KV_HEADS = 2
Q_DIM = N_HEADS * HEAD_DIM
KV_DIM = N_KV_HEADS * HEAD_DIM
ROPE_THETA = 10000.0
Q_BLOCK = 128
LN_EPS = 1e-5
RMS_EPS = 1e-6
ALPHA = (2.0 * DEPTH) ** 0.25
BETA = (8.0 * DEPTH) ** -0.25
N_A = (DEPTH + 1) // 2
N_B = DEPTH // 2


def layer_norm(x, g, b):
    xf = x.astype(jnp.float32)
    mu = jnp.mean(xf, axis=-1, keepdims=True)
    var = jnp.mean(jnp.square(xf - mu), axis=-1, keepdims=True)
    return ((xf - mu) * lax.rsqrt(var + LN_EPS) * g + b).astype(x.dtype)

def rms_norm(x, g):
    xf = x.astype(jnp.float32)
    return (xf * lax.rsqrt(jnp.mean(jnp.square(xf), axis=-1, keepdims=True) + RMS_EPS) * g).astype(x.dtype)

def modulation(cond, w_mod, b_mod):
    m = jax.nn.silu(cond) @ w_mod + b_mod
    return jnp.split(m[..., None, :], N_MOD, axis=-1)

def modulate(x, shift, scale):
    return x * (1.0 + scale) + shift

def swiglu(h, w_in, w_out):
    g, u = jnp.split(h @ w_in, 2, axis=-1)
    return (jax.nn.silu(g) * u) @ w_out

def ffn_sublayer(x, shift, scale, gate, w_in, w_out, ln_g, ln_b):
    y = swiglu(modulate(x, shift, scale), w_in, w_out)
    return layer_norm(ALPHA * x + 0.5 * gate * y, ln_g, ln_b)

def gmlp_mix(h, w_in, sgu_g, sgu_b, w_s, b_s, w_out):
    b_, t_, _ = h.shape
    u, v = jnp.split(jax.nn.gelu(h @ w_in, approximate=False), 2, axis=-1)
    v = layer_norm(v, sgu_g, sgu_b)
    v = v.reshape(b_, t_ // CHUNK, CHUNK, GMLP_GROUPS, GMLP_HALF // GMLP_GROUPS)
    v = jnp.einsum('gpq,bnqgc->bnpgc', w_s, v) + b_s.T[None, None, :, :, None]
    return (u * v.reshape(b_, t_, GMLP_HALF)) @ w_out

def rope_tables(rows, cols):
    quarter = HEAD_DIM // 4
    freqs = ROPE_THETA ** (-jnp.arange(quarter, dtype=jnp.float32) / quarter)
    ang = jnp.concatenate([rows.astype(jnp.float32)[:, None] * freqs,
                           cols.astype(jnp.float32)[:, None] * freqs], axis=-1)
    return jnp.cos(ang), jnp.sin(ang)

def apply_rope(x, cos, sin):
    x1, x2 = jnp.split(x, 2, axis=-1)
    out = jnp.concatenate([x1 * cos - x2 * sin, x2 * cos + x1 * sin], axis=-1)
    return out.astype(x.dtype)

def split_heads(x, n):
    b_, t_, _ = x.shape
    return x.reshape(b_, t_, n, HEAD_DIM).transpose(0, 2, 1, 3)

def merge_heads(x):
    b_, h_, t_, d_ = x.shape
    return x.transpose(0, 2, 1, 3).reshape(b_, t_, h_ * d_)

def attend(q, k, v):
    b_, h_, tq, hd = q.shape
    qg = q.reshape(b_, N_KV_HEADS, h_ // N_KV_HEADS, tq, hd)
    s = jnp.einsum('bkgqd,bktd->bkgqt', qg, k, preferred_element_type=jnp.float32) * (hd ** -0.5)
    p = jax.nn.softmax(s, axis=-1)
    o = jnp.einsum('bkgqt,bktd->bkgqd', p.astype(v.dtype), v)
    return o.reshape(b_, h_, tq, hd)

def block_attend(q, k, v):
    b_, h_, t_, hd = q.shape
    nb = t_ // Q_BLOCK
    qb = q.reshape(b_, h_, nb, Q_BLOCK, hd).transpose(2, 0, 1, 3, 4)
    ob = lax.map(lambda qblk: attend(qblk, k, v), qb)
    return ob.transpose(1, 2, 0, 3, 4).reshape(b_, h_, t_, hd)

def gqa_mix(h_lat, h_ctx, w_qkv, q_norm_g, k_norm_g, w_o, cos, sin, with_ctx_out):
    kv_c = h_ctx @ w_qkv[:, Q_DIM:]
    k_c = rms_norm(split_heads(kv_c[..., :KV_DIM], N_KV_HEADS), k_norm_g)
    v_c = split_heads(kv_c[..., KV_DIM:], N_KV_HEADS)
    qkv = h_lat @ w_qkv
    q_l = apply_rope(rms_norm(split_heads(qkv[..., :Q_DIM], N_HEADS), q_norm_g), cos, sin)
    k_l = apply_rope(rms_norm(split_heads(qkv[..., Q_DIM:Q_DIM + KV_DIM], N_KV_HEADS), k_norm_g), cos, sin)
    v_l = split_heads(qkv[..., Q_DIM + KV_DIM:], N_KV_HEADS)
    k_all = jnp.concatenate([k_c, k_l], axis=2)
    v_all = jnp.concatenate([v_c, v_l], axis=2)
    y_lat = merge_heads(block_attend(q_l, k_all, v_all)) @ w_o
    if not with_ctx_out:
        return y_lat, None
    q_c = rms_norm(split_heads(h_ctx @ w_qkv[:, :Q_DIM], N_HEADS), q_norm_g)
    y_ctx = merge_heads(attend(q_c, k_c, v_c)) @ w_o
    return y_lat, y_ctx

def first_inputs(seed: int = 0) -> dict:
    key = jax.random.key(seed)
    ks = jax.random.split(key, 20)
    f32 = jnp.float32
    nrm = lambda k, shape, s: jax.random.normal(k, shape, f32) * s
    return {
        "x": nrm(ks[0], (BATCH, SEQ, D_MODEL), 1.0),
        "c": nrm(ks[1], (BATCH, D_MODEL), 1.0),
        "ctx": nrm(ks[2], (BATCH, CTX_LEN, D_MODEL), 1.0),
        "c_ctx": nrm(ks[3], (D_MODEL,), 1.0),
        "w_mod": nrm(ks[4], (DEPTH, D_MODEL, N_MOD * D_MODEL), D_MODEL ** -0.5),
        "b_mod": nrm(ks[5], (DEPTH, N_MOD * D_MODEL), 0.02),
        "ln_g": 1.0 + nrm(ks[6], (DEPTH, 3, D_MODEL), 0.02),
        "ln_b": nrm(ks[7], (DEPTH, 3, D_MODEL), 0.02),
        "ffn_w_in": nrm(ks[8], (DEPTH, 2, D_MODEL, 2 * D_FF), D_MODEL ** -0.5),
        "ffn_w_out": nrm(ks[9], (DEPTH, 2, D_FF, D_MODEL), BETA * D_FF ** -0.5),
        "gmlp_w_in": nrm(ks[10], (N_A, D_MODEL, GMLP_D_FF), D_MODEL ** -0.5),
        "gmlp_ln_g": 1.0 + nrm(ks[11], (N_A, GMLP_HALF), 0.02),
        "gmlp_ln_b": nrm(ks[12], (N_A, GMLP_HALF), 0.02),
        "gmlp_w_s": nrm(ks[13], (N_A, GMLP_GROUPS, CHUNK, CHUNK), CHUNK ** -0.5),
        "gmlp_b_s": 1.0 + nrm(ks[14], (N_A, GMLP_GROUPS, CHUNK), 0.02),
        "gmlp_w_out": nrm(ks[15], (N_A, GMLP_HALF, D_MODEL), BETA * GMLP_HALF ** -0.5),
        "attn_w_qkv": nrm(ks[16], (N_B, D_MODEL, Q_DIM + 2 * KV_DIM), D_MODEL ** -0.5),
        "attn_q_norm": 1.0 + nrm(ks[17], (N_B, HEAD_DIM), 0.02),
        "attn_k_norm": 1.0 + nrm(ks[18], (N_B, HEAD_DIM), 0.02),
        "attn_w_o": nrm(ks[19], (N_B, Q_DIM, D_MODEL), BETA * Q_DIM ** -0.5),
    }

def first_block(x, c, ctx, c_ctx, w_mod, b_mod, ln_g, ln_b, ffn_w_in, ffn_w_out,
              gmlp_w_in, gmlp_ln_g, gmlp_ln_b, gmlp_w_s, gmlp_b_s, gmlp_w_out,
              attn_w_qkv, attn_q_norm, attn_k_norm, attn_w_o):
    n_tok = x.shape[1]
    ROWS = n_tok // GRID_W
    rows = jnp.repeat(jnp.arange(ROWS, dtype=jnp.int32), GRID_W)
    cols = jnp.tile(jnp.arange(GRID_W, dtype=jnp.int32), ROWS)
    cos, sin = rope_tables(rows, cols)

    x_lat, x_ctx = x, ctx
    for i in range(DEPTH):
        is_attn = (i % N_MIXERS) == 1
        j = i // N_MIXERS
        last = i == DEPTH - 1
        ctx_feeds_mixer = (not last) or is_attn
        m_lat = modulation(c, w_mod[i], b_mod[i])
        m_ctx = modulation(c_ctx, w_mod[i], b_mod[i])

        x_lat = ffn_sublayer(x_lat, m_lat[0], m_lat[1], m_lat[2],
                             ffn_w_in[i, 0], ffn_w_out[i, 0], ln_g[i, 0], ln_b[i, 0])
        if ctx_feeds_mixer:
            x_ctx = ffn_sublayer(x_ctx, m_ctx[0], m_ctx[1], m_ctx[2],
                                 ffn_w_in[i, 0], ffn_w_out[i, 0], ln_g[i, 0], ln_b[i, 0])

        h_lat = modulate(x_lat, m_lat[3], m_lat[4])
        if is_attn:
            h_ctx = modulate(x_ctx, m_ctx[3], m_ctx[4])
            y_lat, y_ctx = gqa_mix(h_lat, h_ctx, attn_w_qkv[j], attn_q_norm[j], attn_k_norm[j],
                                   attn_w_o[j], cos, sin, not last)
        else:
            y_lat = gmlp_mix(h_lat, gmlp_w_in[j], gmlp_ln_g[j], gmlp_ln_b[j],
                             gmlp_w_s[j], gmlp_b_s[j], gmlp_w_out[j])
            y_ctx = None
            if not last:
                h_ctx = modulate(x_ctx, m_ctx[3], m_ctx[4])
                y_ctx = gmlp_mix(h_ctx, gmlp_w_in[j], gmlp_ln_g[j], gmlp_ln_b[j],
                                 gmlp_w_s[j], gmlp_b_s[j], gmlp_w_out[j])
        x_lat = layer_norm(ALPHA * x_lat + m_lat[5] * y_lat, ln_g[i, 1], ln_b[i, 1])
        if not last:
            x_ctx = layer_norm(ALPHA * x_ctx + m_ctx[5] * y_ctx, ln_g[i, 1], ln_b[i, 1])

        x_lat = ffn_sublayer(x_lat, m_lat[6], m_lat[7], m_lat[8],
                             ffn_w_in[i, 1], ffn_w_out[i, 1], ln_g[i, 2], ln_b[i, 2])
        if not last:
            x_ctx = ffn_sublayer(x_ctx, m_ctx[6], m_ctx[7], m_ctx[8],
                                 ffn_w_in[i, 1], ffn_w_out[i, 1], ln_g[i, 2], ln_b[i, 2])
    return x_lat


EPS = 1e-6
NEG_INF = -1e30
HEAD_DIM_2 = 64
ATT_HEADS = 8
ATT_WIDTH = ATT_HEADS * HEAD_DIM_2
MOBA_BLOCK = 256
MOBA_TOPK = 3
MOBA_Q_CHUNK = 32
CONV_WIDTH = 256
CONV_GROUPS = 4
CONV_KERNEL = 31
GLA_HEADS = 4
GLA_DK = 64
GLA_DV = 64
GLA_KWIDTH = GLA_HEADS * GLA_DK
GLA_VWIDTH = GLA_HEADS * GLA_DV
GLA_GATE_RANK = 16
GLA_TAU = 16.0
GLA_CHUNK = 64
MIX_WIDTH = ATT_WIDTH + CONV_WIDTH + GLA_VWIDTH
IN_WIDTH = 3 * ATT_WIDTH + 2 * CONV_WIDTH + 2 * GLA_KWIDTH + 2 * GLA_VWIDTH + GLA_GATE_RANK
FFN_RES = 0.5


def _rmsnorm(x, gain):
    x32 = x.astype(jnp.float32)
    y = x32 * lax.rsqrt(jnp.mean(x32 * x32, axis=-1, keepdims=True) + EPS)
    return (y * gain.astype(jnp.float32)).astype(x.dtype)

def _layernorm(x, gain, bias):
    x32 = x.astype(jnp.float32)
    mu = jnp.mean(x32, axis=-1, keepdims=True)
    xc = x32 - mu
    y = xc * lax.rsqrt(jnp.mean(xc * xc, axis=-1, keepdims=True) + EPS)
    return (y * gain.astype(jnp.float32) + bias.astype(jnp.float32)).astype(x.dtype)

def _modulate(h, shift, scale):
    return h * (1 + scale[:, None, :]) + shift[:, None, :]

def _swiglu(h, w_in, w_out):
    a, b = jnp.split(h @ w_in, 2, axis=-1)
    return (jax.nn.silu(a) * b) @ w_out

def _split_heads(t, n_heads):
    bsz, seq, _ = t.shape
    return t.reshape(bsz, seq, n_heads, -1).transpose(0, 2, 1, 3)

def _merge_heads(t):
    bsz, n_h, seq, hd = t.shape
    return t.transpose(0, 2, 1, 3).reshape(bsz, seq, n_h * hd)

def _rope_tables(positions):
    inv_freq = 1.0 / (ROPE_THETA ** (jnp.arange(0, HEAD_DIM_2, 2, dtype=jnp.float32) / HEAD_DIM_2))
    ang = positions.astype(jnp.float32)[:, :, None] * inv_freq
    return jnp.cos(ang)[:, None], jnp.sin(ang)[:, None]

def _rope(t, cos, sin):
    t32 = t.astype(jnp.float32)
    t1, t2 = jnp.split(t32, 2, axis=-1)
    return jnp.concatenate([t1 * cos - t2 * sin, t2 * cos + t1 * sin], axis=-1).astype(t.dtype)

def _moba_attention(q, k, v):
    bsz, n_h, seq, hd = q.shape
    n_blk = -(-seq // MOBA_BLOCK)
    pad = n_blk * MOBA_BLOCK - seq
    widths = ((0, 0), (0, 0), (0, pad), (0, 0))
    kb = jnp.pad(k, widths).reshape(bsz, n_h, n_blk, MOBA_BLOCK, hd)
    vb = jnp.pad(v, widths).reshape(bsz, n_h, n_blk, MOBA_BLOCK, hd)
    k_mean = jnp.mean(kb.astype(jnp.float32), axis=3)
    gate = jnp.einsum('bhsd,bhnd->bhsn', q.astype(jnp.float32), k_mean)
    q_blk = jnp.arange(seq) // MOBA_BLOCK
    past = jnp.arange(n_blk)[None, :] < q_blk[:, None]
    gate = jnp.where(past, gate, NEG_INF)
    n_sel = min(MOBA_TOPK, n_blk)
    _, sel = lax.top_k(gate, n_sel)
    sel_ok = sel < q_blk[:, None]
    b_ix = jnp.arange(bsz)[:, None, None, None]
    h_ix = jnp.arange(n_h)[None, :, None, None]
    scale = hd ** -0.5
    qc_len = MOBA_Q_CHUNK

    def one_chunk(ci):
        t0 = ci * qc_len
        blk = t0 // MOBA_BLOCK
        qc = lax.dynamic_slice_in_dim(q, t0, qc_len, axis=2)
        sc = lax.dynamic_slice_in_dim(sel, t0, qc_len, axis=2)
        okc = lax.dynamic_slice_in_dim(sel_ok, t0, qc_len, axis=2)
        k_own = lax.dynamic_index_in_dim(kb, blk, axis=2, keepdims=False)
        v_own = lax.dynamic_index_in_dim(vb, blk, axis=2, keepdims=False)
        k_sel = kb[b_ix, h_ix, sc]
        v_sel = vb[b_ix, h_ix, sc]
        s_own = jnp.einsum('bhqd,bhld->bhql', qc, k_own).astype(jnp.float32) * scale
        q_pos = t0 + jnp.arange(qc_len)
        k_pos = blk * MOBA_BLOCK + jnp.arange(MOBA_BLOCK)
        s_own = jnp.where(k_pos[None, :] <= q_pos[:, None], s_own, NEG_INF)
        s_sel = jnp.einsum('bhqd,bhqnld->bhqnl', qc, k_sel).astype(jnp.float32) * scale
        s_sel = jnp.where(okc[..., None], s_sel, NEG_INF)
        s_all = jnp.concatenate([s_own, s_sel.reshape(bsz, n_h, qc_len, n_sel * MOBA_BLOCK)], axis=-1)
        p = jax.nn.softmax(s_all, axis=-1).astype(v.dtype)
        p_own = p[..., :MOBA_BLOCK]
        p_sel = p[..., MOBA_BLOCK:].reshape(bsz, n_h, qc_len, n_sel, MOBA_BLOCK)
        return (jnp.einsum('bhql,bhld->bhqd', p_own, v_own)
                + jnp.einsum('bhqnl,bhqnld->bhqd', p_sel, v_sel))

    out = lax.map(one_chunk, jnp.arange(seq // qc_len))
    return out.transpose(1, 2, 0, 3, 4).reshape(bsz, n_h, seq, hd)

def _conformer_conv(u, w_dw, b_dw, gain, bias):
    a, g = jnp.split(u, 2, axis=-1)
    h = a * jax.nn.sigmoid(g)
    h = lax.conv_general_dilated(h, w_dw[:, None, :], (1,), [(CONV_KERNEL - 1, 0)],
                                 dimension_numbers=('NWC', 'WIO', 'NWC'),
                                 feature_group_count=CONV_WIDTH) + b_dw
    bsz, seq, ch = h.shape
    hg = h.reshape(bsz, seq, CONV_GROUPS, ch // CONV_GROUPS)
    hg = _layernorm(hg, gain.reshape(CONV_GROUPS, -1), bias.reshape(CONV_GROUPS, -1))
    return jax.nn.silu(hg.reshape(bsz, seq, ch))

def _gla(q, k, v, g):
    bsz, n_h, seq, dk = q.shape
    dv = v.shape[-1]
    L = GLA_CHUNK
    n_c = seq // L
    f32 = jnp.float32
    qc = (q.astype(f32) * dk ** -0.5).reshape(bsz, n_h, n_c, L, dk)
    kc = k.astype(f32).reshape(bsz, n_h, n_c, L, dk)
    vc = v.astype(f32).reshape(bsz, n_h, n_c, L, dv)
    G = lax.cumsum(g.astype(f32).reshape(bsz, n_h, n_c, L, dk), axis=3)
    q_t = qc * jnp.exp(G)
    k_t = kc * jnp.exp(-G)
    causal = jnp.tril(jnp.ones((L, L), dtype=bool))
    A = jnp.where(causal, jnp.einsum('bhnld,bhnmd->bhnlm', q_t, k_t), 0.0)
    o_intra = jnp.einsum('bhnlm,bhnmv->bhnlv', A, vc)
    G_last = G[:, :, :, -1]
    k_end = kc * jnp.exp(G_last[:, :, :, None, :] - G)
    kv = jnp.einsum('bhnld,bhnlv->bhndv', k_end, vc)

    def step(state, inp):
        decay, kv_n = inp
        return decay[..., None] * state + kv_n, state

    init = jnp.zeros((bsz, n_h, dk, dv), f32)
    _, s_prev = lax.scan(step, init, (jnp.moveaxis(jnp.exp(G_last), 2, 0), jnp.moveaxis(kv, 2, 0)))
    s_prev = jnp.moveaxis(s_prev, 0, 2)
    o_inter = jnp.einsum('bhnld,bhndv->bhnlv', q_t, s_prev)
    return (o_intra + o_inter).reshape(bsz, n_h, seq, dv).astype(v.dtype)

def second_inputs(seed: int = 0) -> dict:
    key = jax.random.key(seed)
    ks = jax.random.split(key, 24)
    f32 = jnp.float32

    def nrm(k, shape, s):
        return jax.random.normal(k, shape, f32) * s

    def gain(k, shape):
        return 1.0 + 0.05 * jax.random.normal(k, shape, f32)

    offset = jax.random.randint(ks[2], (BATCH, 1), 0, 1024, dtype=jnp.int32)
    positions = (offset + jnp.arange(SEQ, dtype=jnp.int32)[None, :]).astype(jnp.int32)
    return {
        "x": nrm(ks[0], (BATCH, SEQ, D_MODEL), 1.0),
        "c": nrm(ks[1], (BATCH, D_MODEL), 1.0),
        "positions": positions,
        "ada_w": nrm(ks[3], (DEPTH, D_MODEL, N_MOD * D_MODEL), 0.5 * D_MODEL ** -0.5),
        "ada_b": nrm(ks[4], (DEPTH, N_MOD * D_MODEL), 0.02),
        "ffn1_norm": gain(ks[5], (DEPTH, D_MODEL)),
        "ffn1_w_in": nrm(ks[6], (DEPTH, D_MODEL, 2 * D_FF), D_MODEL ** -0.5),
        "ffn1_w_out": nrm(ks[7], (DEPTH, D_FF, D_MODEL), D_FF ** -0.5),
        "mix_norm": gain(ks[8], (DEPTH, D_MODEL)),
        "mix_w_in": nrm(ks[9], (DEPTH, D_MODEL, IN_WIDTH), D_MODEL ** -0.5),
        "q_norm": gain(ks[10], (DEPTH, HEAD_DIM_2)),
        "k_norm": gain(ks[11], (DEPTH, HEAD_DIM_2)),
        "conv_w": nrm(ks[12], (DEPTH, CONV_KERNEL, CONV_WIDTH), CONV_KERNEL ** -0.5),
        "conv_b": nrm(ks[13], (DEPTH, CONV_WIDTH), 0.02),
        "conv_norm_g": gain(ks[14], (DEPTH, CONV_WIDTH)),
        "conv_norm_b": nrm(ks[15], (DEPTH, CONV_WIDTH), 0.02),
        "gla_gate_w": nrm(ks[16], (DEPTH, GLA_GATE_RANK, GLA_KWIDTH), GLA_GATE_RANK ** -0.5),
        "gla_gate_b": nrm(ks[17], (DEPTH, GLA_KWIDTH), 0.1),
        "gla_out_norm": gain(ks[18], (DEPTH, GLA_DV)),
        "mix_w_out": nrm(ks[19], (DEPTH, MIX_WIDTH, D_MODEL), MIX_WIDTH ** -0.5),
        "ffn2_norm": gain(ks[20], (DEPTH, D_MODEL)),
        "ffn2_w_in": nrm(ks[21], (DEPTH, D_MODEL, 2 * D_FF), D_MODEL ** -0.5),
        "ffn2_w_out": nrm(ks[22], (DEPTH, D_FF, D_MODEL), D_FF ** -0.5),
    }

def second_block(x, c, positions, ada_w, ada_b, ffn1_norm, ffn1_w_in, ffn1_w_out, mix_norm, mix_w_in,
              q_norm, k_norm, conv_w, conv_b, conv_norm_g, conv_norm_b, gla_gate_w, gla_gate_b,
              gla_out_norm, mix_w_out, ffn2_norm, ffn2_w_in, ffn2_w_out):
    cos, sin = _rope_tables(positions)
    c_act = jax.nn.silu(c)
    splits = list(np.cumsum([ATT_WIDTH, ATT_WIDTH, ATT_WIDTH, 2 * CONV_WIDTH,
                             GLA_KWIDTH, GLA_KWIDTH, GLA_VWIDTH, GLA_VWIDTH]))
    for l in range(DEPTH):
        mod = c_act @ ada_w[l] + ada_b[l]
        sh1, sc1, gt1, sh2, sc2, gt2, sh3, sc3, gt3 = jnp.split(mod, N_MOD, axis=-1)

        h = _modulate(_rmsnorm(x, ffn1_norm[l]), sh1, sc1)
        x = x + FFN_RES * gt1[:, None, :] * _swiglu(h, ffn1_w_in[l], ffn1_w_out[l])

        h = _modulate(_rmsnorm(x, mix_norm[l]), sh2, sc2)
        proj = h @ mix_w_in[l]
        a_q, a_k, a_v, b_u, c_q, c_k, c_v, c_r, c_g = jnp.split(proj, splits, axis=-1)

        qa = _rope(_rmsnorm(_split_heads(a_q, ATT_HEADS), q_norm[l]), cos, sin)
        ka = _rope(_rmsnorm(_split_heads(a_k, ATT_HEADS), k_norm[l]), cos, sin)
        va = _split_heads(a_v, ATT_HEADS)
        o_a = _merge_heads(_moba_attention(qa, ka, va))

        o_b = _conformer_conv(b_u, conv_w[l], conv_b[l], conv_norm_g[l], conv_norm_b[l])

        log_decay = jax.nn.log_sigmoid(c_g @ gla_gate_w[l] + gla_gate_b[l]) / GLA_TAU
        o_c = _gla(_split_heads(c_q, GLA_HEADS), _split_heads(c_k, GLA_HEADS),
                   _split_heads(c_v, GLA_HEADS), _split_heads(log_decay, GLA_HEADS))
        o_c = _merge_heads(_rmsnorm(o_c, gla_out_norm[l])) * jax.nn.silu(c_r)

        mixed = jnp.concatenate([o_a, o_b, o_c], axis=-1) @ mix_w_out[l]
        x = x + gt2[:, None, :] * mixed

        h = _modulate(_rmsnorm(x, ffn2_norm[l]), sh3, sc3)
        x = x + FFN_RES * gt3[:, None, :] * _swiglu(h, ffn2_w_in[l], ffn2_w_out[l])
    return x


def setup_inputs(seed=0):
    out = dict(first_inputs(seed))
    for name, value in second_inputs(seed + 1).items():
        if name != "x":
            out[name + "_2"] = value
    return out


def reference(
    x, c, ctx, c_ctx, w_mod, b_mod, ln_g, ln_b, ffn_w_in, ffn_w_out, gmlp_w_in, gmlp_ln_g,
    gmlp_ln_b, gmlp_w_s, gmlp_b_s, gmlp_w_out, attn_w_qkv, attn_q_norm, attn_k_norm, attn_w_o,
    c_2, positions_2, ada_w_2, ada_b_2, ffn1_norm_2, ffn1_w_in_2, ffn1_w_out_2, mix_norm_2,
    mix_w_in_2, q_norm_2, k_norm_2, conv_w_2, conv_b_2, conv_norm_g_2, conv_norm_b_2,
    gla_gate_w_2, gla_gate_b_2, gla_out_norm_2, mix_w_out_2, ffn2_norm_2, ffn2_w_in_2,
    ffn2_w_out_2,
):
    x = first_block(
        x, c, ctx, c_ctx, w_mod, b_mod, ln_g, ln_b, ffn_w_in, ffn_w_out, gmlp_w_in, gmlp_ln_g,
        gmlp_ln_b, gmlp_w_s, gmlp_b_s, gmlp_w_out, attn_w_qkv, attn_q_norm, attn_k_norm,
        attn_w_o,
    )
    return second_block(
        x, c_2, positions_2, ada_w_2, ada_b_2, ffn1_norm_2, ffn1_w_in_2, ffn1_w_out_2,
        mix_norm_2, mix_w_in_2, q_norm_2, k_norm_2, conv_w_2, conv_b_2, conv_norm_g_2,
        conv_norm_b_2, gla_gate_w_2, gla_gate_b_2, gla_out_norm_2, mix_w_out_2, ffn2_norm_2,
        ffn2_w_in_2, ffn2_w_out_2,
    )


_drawn_inputs = setup_inputs


def setup_inputs(seed=0):
    import zlib

    import numpy as np

    out = dict(_drawn_inputs(seed))
    spreads = {}
    factors = {'ctx': 4.063,
     'b_mod': 3.234,
     'gmlp_ln_g': 8.0,
     'gmlp_ln_b': 8.0,
     'gmlp_b_s': 8.0,
     'attn_q_norm': 8.0,
     'attn_k_norm': 8.0,
     'ffn1_norm_2': 5.497,
     'mix_norm_2': 3.299,
     'q_norm_2': 8.0,
     'k_norm_2': 8.0,
     'conv_b_2': 8.0,
     'conv_norm_g_2': 19.009,
     'conv_norm_b_2': 49.742,
     'gla_gate_b_2': 7.935,
     'gla_out_norm_2': 7.383,
     'ffn2_norm_2': 5.323}
    for name, (base, spread) in spreads.items():
        noise = np.random.default_rng([zlib.crc32(name.encode()), seed]).standard_normal(out[name].shape)
        drawn = base * np.exp(spread * noise) if base else spread * noise
        out[name] = __import__('jax').numpy.asarray(drawn.astype(out[name].dtype))
    for name, factor in factors.items():
        out[name] = (out[name] * factor).astype(out[name].dtype)
    return out
```

```python
from contextlib import ExitStack

import numpy as np
import concourse.bass as bass
from concourse import mybir

P = 128
B2 = 6
F32 = mybir.dt.float32
F32R = mybir.dt.float32r
I32 = mybir.dt.int32
ALU = mybir.AluOpType
ACT = mybir.ActivationFunctionType
AX = mybir.AxisListType

D = 1024
KD = D // P
T = 256
TT = T // P
DEPTH = 2
D_FF = 2816
KF = D_FF // P
GROUPS = (12, 10)
GM_HALF = 3072
GM_GROUP = 768
GM_STEPS = GM_HALF // GM_GROUP
SG_GROUPS = 8
HEADS, KV_HEADS, HD = 8, 2, 128
QKV = (HEADS + 2 * KV_HEADS) * HD
M_HEADS, M_HD = 8, 64
G_HEADS, G_D = 4, 64
IN_W = 3088
CONV_K = 31
ALPHA = (2.0 * DEPTH) ** 0.25
LN_EPS, RMS_EPS = 1e-5, 1e-6
NEG = -1e30
FIRST = 2
ROUND = 1.5 * 2.0 ** 23
TURN = (6.28125, 0.0019350051879882812, 3.019915981956753e-07)
PI_BELOW = 3.1415925
CW = 256


def plan():
    subs = []
    for l in range(DEPTH):
        both = (0, 1)
        last = l == DEPTH - 1
        mixer = "attn" if l % 2 else "gmlp"
        subs.append(dict(block=1, layer=l, kind="ffn", part=0, streams=both, post=both))
        subs.append(dict(block=1, layer=l, kind=mixer, part=1, streams=both, post=(0,) if last else both))
        subs.append(dict(block=1, layer=l, kind="ffn", part=2, streams=(0,) if last else both,
                         post=(0,) if last else both))
    for l in range(DEPTH):
        for part, kind in enumerate(("ffn", "mix", "ffn")):
            subs.append(dict(block=2, layer=l, kind=kind, part=part, streams=(0,), post=(0,)))
    n = dict(unit=FIRST, inq=FIRST, h=FIRST, sg=0, group=0, pre=0, tr=0, item=0, mix=0, tile=0)
    for i, s in enumerate(subs):
        s["i"] = i
        s.update({"n_" + k: v for k, v in n.items()})
        ns = len(s["streams"])
        n["pre"] += ns
        n["tr"] += ns + (s["kind"] in ("attn", "mix"))
        if s["kind"] == "ffn":
            n["unit"] += KF + KF // 2
            n["inq"] += KF
            n["h"] += KF
            n["sg"] += KF
            n["group"] += len(GROUPS)
            n["tile"] += len(GROUPS) * (TT * ns - 1)
        elif s["kind"] == "gmlp":
            n["unit"] += ns * 36
            n["inq"] += ns * 24
            n["h"] += ns * 12
            n["sg"] += ns * 12
            n["group"] += ns
        elif s["kind"] == "attn":
            n["unit"] += 6 + 2 + 4
            n["inq"] += 8
            n["group"] += 1
            n["tile"] += TT - 1
            n["item"] += HEADS * TT
        else:
            n["unit"] += 12 + 4
            n["inq"] += 12
            n["group"] += 1
            n["tile"] += TT - 1
            n["item"] += M_HEADS * TT
            n["mix"] += 1
    return subs


class Items(list):

    def __init__(self, block):
        self.d, self.masked = (HD, False) if block == 1 else (M_HD, True)
        n = HEADS if block == 1 else M_HEADS
        super().__init__((h, t, (t + 1) * P if self.masked else 2 * T) for h in range(n) for t in range(TT))
        self.scale = self.d ** -0.5


class Stages:

    def __init__(self, sem, names):
        self.sem, self.names, self.at = sem, names.split(), 0

    def done(self, name, ins):
        self.skip(name)
        ins.then_inc(self.sem, 1)

    def skip(self, name):
        assert self.names[self.at] == name, (name, self.names[self.at])
        self.at = (self.at + 1) % len(self.names)

    def wait(self, eng, name, turn):
        eng.wait_ge(self.sem, turn * len(self.names) + self.names.index(name) + 1)


class Steps:

    def __init__(self, eng, sem, start=0):
        self.eng, self.sem, self.n, self.loop = eng, sem, start, None

    def value(self, n=None):
        n = self.n if n is None else n
        return n if self.loop is None else n + self.loop[0] * self.loop[1]

    def mark(self, ins):
        ins.then_inc(self.sem, 1)
        self.n += 1
        return self.n

    def wait(self, n):
        self.eng.wait_ge(self.sem, self.value(n))

    def link(self, ins):
        self.wait(self.mark(ins))

    def enter(self, i, each):
        self.loop = (i, each)
        self.first = self.n

    def leave(self, times):
        i, each = self.loop
        assert self.n - self.first == each, (self.n - self.first, each)
        self.n, self.loop = self.first + each * times, None


def program(nc, ins, out, subs):
    u_end = subs[-1]["n_unit"] + dict(ffn=33, gmlp=72, attn=12, mix=16)[subs[-1]["kind"]]
    with ExitStack() as ctx:
        def sb(name, shape, dt=F32):
            return ctx.enter_context(nc.sbuf_tensor(name, shape, dt))

        def sem(name):
            return ctx.enter_context(nc.semaphore(name))

        x = sb("x", [P, 2, TT, D])
        wraw = sb("wraw", [P, 2, 2048])
        wh = sb("wh", [P, 2, 2048], F32R)
        wl = sb("wl", [P, 2, 2048], F32R)
        mraw = sb("mraw", [P, 2, 2, D])
        acc = sb("acc", [P, 2, D])
        biasrow = sb("biasrow", [P, D])
        gate = sb("gate", [P, 2, D])
        lnp = sb("lnp", [P, 2, D])
        modc = sb("modc", [P, 2, 3, 2, KD])
        prea = sb("prea", [P, 2, KD])
        gaincol = sb("gaincol", [P, KD])
        cvec = sb("cvec", [P, 3, KD])
        svec = sb("svec", [P, 3, KD])
        sg = sb("sg", [P, 2, 512])
        ht = sb("ht", [P, 2, 512])
        ident = sb("ident", [P, P])
        ones = sb("ones", [P, P])
        st = sb("st", [P, TT, 12, 6])
        mv = sb("mv", [P, TT, 2])
        rstd = sb("rstd", [P, TT])
        wst = sb("wst", [P, SG_GROUPS, P])
        zeros = sb("zeros", [P, P], F32R)
        scrap = sb("scrap", [P, TT])
        mhalf = sb("mhalf", [P, TT * 16])
        nrm = sb("nrm", [P, TT, 16])
        negm = sb("negm", [P, 16])
        den = sb("den", [P, 2, 16])
        hgain = sb("hgain", [P, 2, HD])
        rope = sb("rope", [P, TT, 2, HD // 2])
        rope2 = sb("rope2", [P, 2, TT, M_HD // 2])
        pos = sb("pos", [P, TT], I32)
        cgh_, cgl_ = sb("cgh", [P, KD * 16], F32R), sb("cgl", [P, KD * 16], F32R)
        cgh, cgl = cgh_[:], cgl_[:]

        def alias(*shapes):
            with ExitStack() as a:
                return [a.enter_context(nc.sbuf_tensor(n, s, d)) for n, s, d in shapes]
        xh, xl = alias(("xh", [P, KD, 2 * T], F32R), ("xl", [P, KD, 2 * T], F32R))
        qt_t, kt_t, qeo, sc_t, kvs, sts, cg_t = alias(
            ("qt_t", [64, G_HEADS, T], F32), ("kt_t", [64, G_HEADS, T], F32), ("qeo", [64, 2, G_HEADS, T], F32),
            ("sc_t", [P, TT * G_HEADS, P], F32), ("kvs", [64, G_HEADS, 4, G_D], F32),
            ("sts", [64, G_HEADS, 3, G_D], F32), ("cg_t", [32, T], F32))
        q2, k2, tm2, ch_t, cacc, ctok, cw_t = alias(
            ("q2", [64, M_HEADS, T], F32), ("k2", [64, M_HEADS, T], F32), ("tm2", [P, 2, 1024], F32),
            ("ch_t", [P, 2, T + 32], F32), ("cacc", [P, 2, T], F32), ("ctok", [P, TT, 256], F32),
            ("cw_t", [P, 2, 32], F32))
        sb("place_of_inputs", [P, 2 * KD * 2 * T])
        hh, hl = alias(("hh", [P, 12 * 512], F32R), ("hl", [P, 12 * 512], F32R))
        _, zt0, _, zt1 = alias(("hh_", [P, 10 * 512], F32), ("zt0", [P, D], F32),
                               ("hl_", [P, 10 * 512], F32), ("zt1", [P, D], F32))
        zt = (zt0, zt1)
        first_w, = alias(("first_w", [P, 6, 2, D], F32))
        ptmp, z = alias(("ptmp", [P, 2, KD, T], F32), ("z", [P, TT, D], F32))
        _, v0, vg, _, v1, gb = alias(("gm_hh", [P, 1536], F32), ("v0", [P, GM_HALF], F32),
                                     ("vg", [P, TT, GM_GROUP], F32), ("gm_hl", [P, 1536], F32),
                                     ("v1", [P, GM_HALF], F32), ("gb", [P, 2, GM_GROUP], F32))
        v = (v0, v1)
        ql, kvc, _, qt1, kt1, tm1 = alias(("ql", [P, TT, QKV], F32), ("kvc", [P, TT, 2 * KV_HEADS * HD], F32),
                                        ("at_z", [P, TT, D], F32), ("qt1", [P, HEADS, T], F32),
                                        ("kt1", [P, KV_HEADS, 2 * T], F32), ("tm1", [P, 2, 1280], F32))
        proj, om, gg, e1, e2, e3, kt, ke = alias(
            ("proj", [P, TT, 3072], F32), ("om", [P, TT, D], F32), ("gg", [P, TT, 256], F32),
            ("e1", [P, TT, 256], F32), ("e2", [P, TT, 256], F32), ("e3", [P, TT, 256], F32),
            ("kt", [P, TT, 256], F32), ("ke", [P, 2, TT, 256], F32))
        bsrow = mraw[0:1, 0, 0]
        ps = ctx.enter_context(nc.psum_tensor("ps", [P, 8, 512], F32))
        place = x[:, 1].rearrange("p t d -> p (t d)")
        causal, tri, suf = (place[:, i * P:(i + 1) * P] for i in range(3))
        conv_raw, gate_raw = place[0:32, 512:768], place[0:32, 768:1024]
        conv_norm = place[:, 1024:1536].rearrange("p (a b) -> p a b", a=2)
        out_norm, cg_raw = place[:, 1536:1600], place[:, 1600:1728]
        cg_tok = place[:, 1728:1760]
        decay = place[0:64, 1760:1776]
        freqs = place[:, 1776:1808]
        hst = place[:, 1808:1856].rearrange("p (a b) -> p a b", a=8)
        hmv = place[:, 1856:1872].rearrange("p (a b) -> p a b", a=8)
        hrs = place[:, 1872:1880]
        tm_ang = place[:, 1880:1944].rearrange("p (t f) -> p t f", t=TT)
        ang = place[:, 384:512].rearrange("p (a t f) -> p a t f", a=2, t=TT)

        wraw_full = [sem("wraw_full0"), sem("wraw_full1")]
        whi_done, wlo_done = sem("whi_done"), sem("wlo_done")
        w_used = sem("w_used")
        mraw_full = [sem("mraw_full0"), sem("mraw_full1")]
        mod_used = sem("mod_used")
        first_full = [sem("first_full%d" % i) for i in range(6)]
        first_used, first_bias, first_rows = sem("first_used"), sem("first_bias"), sem("first_rows")
        bias_full, bias_used = sem("bias_full"), sem("bias_used")
        cols_ready, mcol_done = sem("cols_ready"), sem("mcol_done")
        gate_ps = sem("gate_ps")
        pair_free = sem("pair_free")
        sg_ready, h_ready = sem("sg_ready"), sem("h_ready")
        y_tile = sem("y_tile")
        y_evac = sem("y_evac")
        x_ready, z_ready = sem("x_ready"), sem("z_ready")
        tr_done = sem("tr_done")
        tr_act, tr_dve = sem("tr_act"), sem("tr_dve")
        x_mod = sem("x_mod")
        pre_hi, pre_ready = sem("pre_hi"), sem("pre_ready")
        ssq_ready, var_ready, rstd_ready = sem("ssq_ready"), sem("var_ready"), sem("rstd_ready")
        ln_full, ln_used = sem("ln_full"), sem("ln_used")
        gain_full, gain_used = sem("gain_full"), sem("gain_used")
        in_full, ident_ready, svec_ready = sem("in_full"), sem("ident_ready"), sem("svec_ready")
        vstep, pstep, astep = sem("vstep"), sem("pstep"), sem("astep")
        out_full = sem("out_full")
        ws_full, ws_read, wst_ps, wst_ready = sem("ws_full"), sem("ws_read"), sem("wst_ps"), sem("wst_ready")
        bs_full, y_closed = sem("bs_full"), sem("y_closed")
        gb_full, gb_used, vg_ready = sem("gb_full"), sem("gb_used"), sem("vg_ready")
        s_ps, max_ready, p_ready = sem("s_ps"), sem("max_ready"), sem("p_ready")
        pt_ps, pt_ready = sem("pt_ps"), sem("pt_ready")
        o_ps, o_taken = sem("o_ps"), sem("o_taken")
        att_full = sem("att_full")
        AA = Stages(sem("attention_act"), "heads")
        AV = Stages(sem("attention_dve"), "shaped heads")
        AP_ = Stages(sem("attention_pe"), "heads")
        mix_full, ang_ready, rope2_ready = sem("mix_full"), sem("ang_ready"), sem("rope2_ready")
        MA = Stages(sem("mix_act"), "cgh softplus decays qt_t silu sig q2 conv")
        MV = Stages(sem("mix_dve"), "cgl cgt cg_t absz g qk kt_t states oc h shaped k2 ch_t taps stats o_conv")
        MP = Stages(sem("mix_pe"), "cg cg_t z sums qk_t scores o heads h_t conv")
        MG = Stages(sem("mix_pool"), "masks")
        block = ctx.enter_context(nc.Block())

        def mod_of(s):
            w, b = ("w_mod", "b_mod") if s["block"] == 1 else ("ada_w_2", "ada_b_2")
            return ins[w][s["layer"]].rearrange("(p j) n -> p j n", j=KD), ins[b], 3 * D * s["part"]

        def conds(s):
            return (0, 1)[:len(s["streams"])]

        def ffn_w(s):
            l = s["layer"]
            if s["block"] == 1:
                return ins["ffn_w_in"][l, s["part"] // 2], ins["ffn_w_out"][l, s["part"] // 2]
            n = "ffn1" if s["part"] == 0 else "ffn2"
            return ins[n + "_w_in_2"][l], ins[n + "_w_out_2"][l]

        def mods_taken(per, j, i):
            return [(i, q) for q in ((0, 1), (2,), (3,), ())[j]] if per == 4 else [(j // 2, 2 * (j % 2) + q) for q in (0, 1)]

        def mods_loaded(per, j, i):
            if per == 4:
                return [(i, q) for q in ((0,), (1,), (), (2, 3))[j]]
            n = j - 2 if j else 0
            return [] if j in (1, 2) else mods_taken(per, n, i)

        def section_done(per, j, i):
            return (i if j == per - 1 else None) if per == 4 else (j // 2 if j % 2 else None)

        def after(s):
            return subs[s["i"] + 1] if s["i"] + 1 < len(subs) else None

        def loop(eng, n, per, body, steps=None, each=0):
            turns = n // per
            if turns > 1:
                with eng.Fori(0, turns) as i:
                    if steps:
                        steps.enter(i, each)
                    for j in range(per):
                        body(i * per + j, j, i)
                if steps:
                    steps.leave(turns)
            else:
                for j in range(turns * per):
                    body(j, j, 0)
            for j in range(n - turns * per):
                body(turns * per + j, j, turns)

        def split_steps(n, u0, per):
            return (n - per, per) if u0 + n == u_end else (n, 0)

        @block.sync
        def _(sp):
            unit = [FIRST]

            def load_mod(s, sec, q, mu):
                w, b, off = mod_of(s)
                if q == 0:
                    sp.wait_ge(bias_used, sec + (3 * s["i"] + 1))
                    sp.dma_start(biasrow[0:1, :], b[s["layer"]:s["layer"] + 1, bass.ds(sec * D + off, D)])\
                        .then_inc(bias_full, 16)
                sp.wait_ge(mod_used, mu)
                sp.dma_start(mraw[:, q % 2], w[:, 2 * q:2 * q + 2, bass.ds(sec * D + off, D)])\
                    .then_inc(mraw_full[q % 2], 16)

            def load(u, count, halves, by_column=False):
                slot = u % 2
                sp.wait_ge(wlo_done, count)
                for half, a in enumerate(halves):
                    n_a, n_b = a.shape[1], a.shape[2]
                    if by_column:
                        dst = wraw[:, slot].rearrange("p (a t b) -> p a t b", t=2, b=n_b)[:, :, half]
                    else:
                        dst = wraw[:, slot, half * n_a * n_b:(half + 1) * n_a * n_b]\
                            .rearrange("p (a b) -> p a b", a=n_a)
                    sp.dma_start(dst, a).then_inc(wraw_full[slot], 16)

            def phase(n, per, src, mods=None, by_column=False):
                u0 = unit[0]

                def body(idx, j, i):
                    load(u0 + j, idx + u0, src(idx), by_column)
                    if mods is not None:
                        for sec, q in mods_loaded(per, j, i):
                            load_mod(mods, sec, q, sec * 4 + (12 * mods["i"] + q + 1))
                loop(sp, n, per, body)
                unit[0] += n

            for full in wraw_full:
                sp.sem_inc(full, 16 * FIRST)
            for full in mraw_full:
                sp.sem_inc(full, 64)
            sp.sem_inc(bias_full, 32)
            for k, name in enumerate(("c", "c_ctx", "c_2")):
                v = ins[name]
                v = v.rearrange("a n -> (a n)") if len(v.shape) == 2 else v
                sp.dma_start(cvec[:, k], v.rearrange("(p j) -> p j", j=KD)).then_inc(in_full, 16)
            sp.dma_start(x[:, 0], ins["x"][0].rearrange("(t p) d -> p t d", p=P)).then_inc(in_full, 16)
            sp.dma_start(x[:, 1], ins["ctx"][0].rearrange("(t p) d -> p t d", p=P)).then_inc(in_full, 16)
            sp.dma_start(ht[:].rearrange("p a b -> p (a b)").rearrange("p (g q) -> p g q", g=SG_GROUPS),
                         ins["gmlp_w_s"][0].rearrange("g p q -> p g q")).then_inc(ws_full, 16)
            w, b, off = mod_of(subs[0])
            sp.dma_start(gate[0:2].rearrange("p a b -> p (a b)"), b[subs[0]["layer"], off:off + 2 * D].partition_broadcast(2))\
                .then_inc(first_bias, 16)
            for n in range(8):
                if n % 2 == 0:
                    load_mod(subs[0], 2, n // 2, n // 2 + 9)
                if n >= 6:
                    sp.wait_ge(first_used, n - 5)
                at = off + n // 4 * D
                sp.dma_start(first_w[:, n % 6], w[:, 2 * (n % 4):2 * (n % 4) + 2, at:at + D]).then_inc(first_full[n % 6], 16)
            for s in subs:
                nxt = after(s)
                if s["kind"] == "ffn":
                    w_in, w_out = ffn_w(s)
                    w_in = w_in.rearrange("(k p) (t m c) -> p k t m c", p=P, t=2, c=P)
                    w_out = w_out.rearrange("(m p) n -> p m n", p=P)
                    m0 = 0
                    for g, n in enumerate(GROUPS):
                        phase(n, 2 if g else 4, lambda idx: [
                            w_in[:, :, t, bass.ds(idx + m0, 1), :].rearrange("p k m c -> p k (m c)")
                            for t in range(2)], None if g else nxt, by_column=True)
                        phase(n // 2, 2, lambda idx: [w_out[:, bass.ds(idx * 2 + (m0 + kk), 1), :] for kk in range(2)])
                        m0 += n
                elif s["kind"] == "gmlp":
                    w_in = ins["gmlp_w_in"][0].rearrange("(k p) n -> p k n", p=P)
                    w_out = ins["gmlp_w_out"][0].rearrange("(m p) n -> p m n", p=P)
                    lng, lnb = ins["gmlp_ln_g"][0], ins["gmlp_ln_b"][0]
                    for k, c in enumerate(s["streams"]):
                        phase(12, 4, lambda idx: [w_in[:, kk:kk + 4, bass.ds(idx * CW + GM_HALF, CW)]
                                                  for kk in (0, 4)], nxt if k == 0 else None)
                        if k == 0:
                            sp.wait_ge(mod_used, 12 * (s["i"] + 2) + 2)
                            sp.dma_start(bsrow, ins["gmlp_b_s"].rearrange("a g p -> a (g p)")).then_inc(bs_full, 16)
                        u0 = unit[0]

                        def group(idx, j, i):
                            sp.wait_ge(gb_used, idx + (GM_STEPS * k + 1))
                            for b, a in enumerate((lng, lnb)):
                                row = a[bass.ds(idx * GM_GROUP, GM_GROUP)].partition_broadcast(P)
                                sp.dma_start(gb[:, b], row).then_inc(gb_full, 16)
                            for q in range(3):
                                load(u0 + q, idx * 6 + (u0 + q),
                                     [w_in[:, kk:kk + 4, bass.ds(idx * GM_GROUP + q * CW, CW)] for kk in (0, 4)])
                            for q in range(3):
                                load(u0 + 3 + q, idx * 6 + (u0 + 3 + q),
                                     [w_out[:, bass.ds(idx * 6 + (2 * q + kk), 1), :] for kk in range(2)])
                        loop(sp, GM_STEPS, 1, group)
                        unit[0] += 6 * GM_STEPS
                    sp.wait_ge(w_used, unit[0])
                elif s["kind"] == "attn":
                    for g, name in enumerate(("attn_q_norm", "attn_k_norm")):
                        sp.dma_start(hgain[:, g], ins[name][0].partition_broadcast(P)).then_inc(att_full, 16)
                    for t in range(TT):
                        sp.dma_start(rope[:, t], ins["rope_1"].rearrange("a (t p) d -> p t a d", p=P)[:, t])\
                            .then_inc(att_full, 16)
                    w_in = ins["attn_w_qkv"][0].rearrange("(k p) n -> p k n", p=P)
                    w_out = ins["attn_w_o"][0].rearrange("(m p) n -> p m n", p=P)
                    phase(8, 8, lambda idx: [w_in[:, kk:kk + 4, bass.ds((idx if idx < 6 else idx - 2) * CW, CW)]
                                             for kk in (0, 4)], nxt)
                    phase(4, 2, lambda idx: [w_out[:, bass.ds(idx * 2 + kk, 1), :] for kk in range(2)])
                elif s["kind"] == "mix":
                    w_in = ins["mix_w_in_2"][s["layer"]].rearrange("(k p) n -> p k n", p=P)
                    w_out = ins["mix_w_out_2"][s["layer"]].rearrange("(m p) n -> p m n", p=P)
                    phase(12, 4, lambda idx: [w_in[:, kk:kk + 4, bass.ds(idx * CW, CW)] for kk in (0, 4)], nxt)
                    phase(4, 2, lambda idx: [w_out[:, bass.ds(idx * 2 + kk, 1), :] for kk in range(2)])
            sp.wait_ge(x_ready, subs[-1]["n_pre"] + len(subs[-1]["streams"]) + 1)
            sp.dma_start(out[0].rearrange("(t p) d -> p t d", p=P), x[:, 0]).then_inc(out_full, 16)
            sp.wait_ge(out_full, 16)

        @block.gpsimd
        def _(pool):
            steps = Steps(pool, pstep)
            steps.link(pool.memset(ident[:], 0.0))
            steps.link(pool.affine_select(out=ident[:], in_=ident[:], compare_op=ALU.not_equal, fill=1.0, base=0,
                                          pattern=[[-1, P]], channel_multiplier=1))
            pool.memset(ones[:], 1.0).then_inc(ident_ready, 1)
            steps.link(pool.memset(mhalf[:], -0.5))
            pool.memset(zeros[:].bitcast(F32), 0.0).then_inc(ident_ready, 1)
            n_power = [0]

            def power(what=rstd[:], n=TT):
                n_power[0] += 1
                pool.wait_ge(var_ready, n_power[0])
                pool.tensor_tensor(what, what, mhalf[:, 0:n], ALU.pow).then_inc(rstd_ready, 1)

            def split(where, par, width):
                steps.link(pool.tensor_copy(hh[:, where], ht[:, par, 0:width]))
                pool.tensor_tensor(hl[:, where], ht[:, par, 0:width], hh[:, where].bitcast(F32), ALU.subtract)\
                    .then_inc(h_ready, 1)

            def split_h(n, q0, h0, width, at):
                def body(idx, j, i):
                    pool.wait_ge(pair_free, idx + (q0 + 2))
                    split(bass.ds(idx * width + at, width), (q0 + j) % 2, width)
                loop(pool, n, 2, body, steps, 2)

            for s in subs:
                if s["block"] == 2:
                    pool.wait_ge(gain_used, s["i"] - B2)
                    g = ins[{0: "ffn1_norm_2", 1: "mix_norm_2", 2: "ffn2_norm_2"}[s["part"]]][s["layer"]]
                    with nc.allow_non_contiguous_dma("a column of 1024 gains"):
                        pool.dma_start(gaincol[:], g.rearrange("(k p) -> p k", p=P)).then_inc(gain_full, 16)
                    power()
                else:
                    pool.wait_ge(ln_used, s["i"])
                    for k, name in enumerate(("ln_g", "ln_b")):
                        pool.dma_start(lnp[:, k], ins[name][s["layer"], s["part"]].partition_broadcast(P))\
                            .then_inc(ln_full, 16)
                if s["kind"] == "ffn":
                    m0 = 0
                    for g, n in enumerate(GROUPS):
                        pool.wait_ge(w_used, s["n_unit"] + 18 * g)
                        split_h(n, s["n_inq"] + m0, s["n_h"] + m0, T * len(s["streams"]), 0)
                        m0 += n
                elif s["kind"] == "gmlp":
                    for k, c in enumerate(s["streams"]):
                        u0, q0 = s["n_unit"] + 36 * k + 12, s["n_inq"] + 24 * k + 12
                        power()

                        def group(idx, j, i):
                            pool.wait_ge(w_used, idx * 6 + u0)
                            for q in range(3):
                                pool.wait_ge(pair_free, idx * 3 + (q0 + q + 2))
                                pool.tensor_tensor(scrap[:], mhalf[:, 0:TT], mhalf[:, 0:TT], ALU.add)
                                split(slice(q * 512, (q + 1) * 512), q % 2, 512)
                        loop(pool, GM_STEPS, 1, group, steps, 3)
                elif s["kind"] == "attn":
                    power(nrm[:].rearrange("p a b -> p (a b)"), TT * 16)
                elif s["kind"] == "mix":
                    turn, l = s["n_mix"], s["layer"]
                    pool.wait_ge(x_ready, s["n_pre"] + 1)
                    loads = [(cg_raw.rearrange("p (k c) -> p k c", k=KD),
                              ins["mix_w_in_2"][l].rearrange("(k p) n -> p k n", p=P)[:, :, 3072:IN_W]),
                             (conv_raw[0:CONV_K], ins["conv_w_2"][l]), (conv_raw[CONV_K:CONV_K + 1], ins["conv_b_2"][l:l + 1]),
                             (gate_raw[0:16], ins["gla_gate_w_2"][l]), (gate_raw[16:17], ins["gla_gate_b_2"][l:l + 1]),
                             (out_norm, ins["gla_out_norm_2"][l].partition_broadcast(P)),
                             (hgain[:, 0, 0:M_HD], ins["q_norm_2"][l].partition_broadcast(P)),
                             (hgain[:, 1, 0:M_HD], ins["k_norm_2"][l].partition_broadcast(P)),
                             (conv_norm[:, 0], ins["conv_norm_g_2"][l].partition_broadcast(P)),
                             (conv_norm[:, 1], ins["conv_norm_b_2"][l].partition_broadcast(P))]
                    if turn == 0:
                        loads += [(pos[:], ins["positions_2"][0].rearrange("(t p) -> p t", p=P)),
                                  (freqs, ins["rope_freqs_2"][0].partition_broadcast(P))]
                    with nc.allow_non_contiguous_dma("small tables"):
                        for to, a in loads:
                            pool.dma_start(to, a).then_inc(mix_full, 16)
                    if turn == 0:
                        pool.memset(causal, 0.0)
                        pool.memset(tri, 1.0)
                        steps.link(pool.memset(suf, 1.0))
                        pool.affine_select(out=causal, in_=causal, compare_op=ALU.is_ge, fill=NEG, base=0,
                                           pattern=[[-1, P]], channel_multiplier=1)
                        pool.affine_select(out=tri, in_=tri, compare_op=ALU.is_ge, fill=0.0, base=0,
                                           pattern=[[1, P]], channel_multiplier=-1)
                        steps.link(pool.affine_select(out=suf, in_=suf, compare_op=ALU.is_ge, fill=0.0, base=-1,
                                                      pattern=[[-1, P]], channel_multiplier=1))
                        pool.memset(tri[0:64, 64:P], 0.0)
                        MG.done("masks", pool.memset(suf[64:P, 0:64], 0.0))
                    else:
                        MG.done("masks", pool.memset(scrap[:], 0.0))
                    power(nrm[:].rearrange("p a b -> p (a b)"), TT * 16)
                    power(nrm[:].rearrange("p a b -> p (a b)"), TT * 16)
                    power(hrs, 8)
                if s["block"] == 1:
                    for c in s["post"]:
                        power()

        @block.scalar
        def _(act):
            steps = Steps(act, astep)

            def split_next(u, i=0, each=0):
                slot = (u + 1) % 2
                act.wait_ge(wraw_full[slot], i * (16 * each) + 32 * ((u + 1) // 2 + 1))
                act.wait_ge(w_used, i * each + u)
                act.activation(wh[:, slot], wraw[:, slot], ACT.Copy).then_inc(whi_done, 1)

            def phase(n, u0, per, evac=None):
                def body(idx, j, i, split=True):
                    if split:
                        split_next(u0 + idx) if isinstance(idx, int) else split_next(u0 + j, i, per)
                    if evac:
                        evac(idx, j, i)
                if u0 + n == u_end:
                    loop(act, n - 1, per, body)
                    body(n - 1, (n - 1) % per, 0, False)
                else:
                    loop(act, n, per, body)

            act.wait_ge(in_full, 5 * 16)
            act.activation(svec[:], cvec[:], ACT.Silu).then_inc(svec_ready, 1)
            act.sem_inc(whi_done, FIRST)
            act.wait_ge(wraw_full[0], 16 * FIRST + 32)
            act.activation(wh[:, 0], wraw[:, 0], ACT.Copy).then_inc(whi_done, 1)

            def prepare_half(s, k, c, source=None):
                r = s["n_tr"] + k
                act.wait_ge(tr_done, r + 1)
                act.wait_ge(x_mod, s["i"] + 1)
                for kc in range(4):
                    last = act.activation(ptmp[:, c, kc], ps[:, kc // 2, (kc % 2) * T:(kc % 2 + 1) * T], ACT.Identity,
                                          bias=modc[:, s["i"] % 2, 0, c, kc:kc + 1], scale=prea[:, c, kc:kc + 1])
                last.then_inc(tr_act, 1)
                split_input(r, c)

            def split_input(r, c):
                for half, ready in enumerate((tr_act, tr_dve)):
                    act.wait_ge(ready, r + 1)
                    act.activation(xh[:, 4 * half:4 * half + 4, c * T:(c + 1) * T], ptmp[:, c, 4 * half:4 * half + 4],
                                   ACT.Copy).then_inc(pre_hi, 1)

            def copies(u0, q0, to):
                def evac(idx, j, i):
                    pair = (q0 + j) % 2
                    act.wait_ge(w_used, idx + (u0 + 1))
                    act.activation(to[:, :, bass.ds(idx * CW, CW)], ps[:, 2 * pair:2 * pair + 2, 0:CW], ACT.Copy)\
                        .then_inc(pair_free, 1)
                return evac

            def exponentials(n0, items):
                for n, (h, t, keys) in enumerate(items):
                    act.wait_ge(max_ready, n0 + n + 1)
                    if n >= 2:
                        act.wait_ge(pt_ps, n0 + n - 1)
                    act.activation(sg[:, n % 2, 0:keys], ps[:, n % 2, 0:keys], ACT.Exp, bias=negm[:, n:n + 1],
                                   scale=items.scale, accum_out=den[:, 0, n:n + 1]).then_inc(p_ready, 1)

            def copy_output(r):
                act.wait_ge(tr_done, r + 1)
                act.activation(ptmp[:, 0, 0:4].rearrange("p a b -> p (a b)"),
                               ps[:, 0:2].rearrange("p a b -> p (a b)"), ACT.Copy).then_inc(tr_act, 1)
                split_input(r, 0)

            for s in subs:
                if s["block"] == 2:
                    act.wait_ge(x_ready, s["n_pre"] + 1)
                    for t in range(TT):
                        act.activation(z[:, t], x[:, 0, t], ACT.Square, accum_out=rstd[:, t:t + 1])\
                            .then_inc(ssq_ready, 1)
                for k, c in enumerate(s["streams"]):
                    prepare_half(s, k, c)
                if s["kind"] == "ffn":
                    W = T * len(s["streams"])
                    m0, u0 = 0, s["n_unit"]
                    for g, n in enumerate(GROUPS):
                        q0 = s["n_inq"] + m0

                        def evac(idx, j, i):
                            pair = (q0 + j) % 2
                            act.wait_ge(w_used, idx + (u0 + 1))
                            act.wait_ge(pair_free, idx + q0)
                            act.activation(sg[:, pair, 0:W], ps[:, 2 * pair, 0:W], ACT.Silu).then_inc(sg_ready, 1)
                        phase(n, u0, 2 if g else 4, evac)
                        phase(n // 2, u0 + n, 2)
                        m0 += n
                        u0 += n + n // 2
                elif s["kind"] == "gmlp":
                    for k, c in enumerate(s["streams"]):
                        u0, q0 = s["n_unit"] + 36 * k, s["n_inq"] + 24 * k

                        def gelu(idx, j, i):
                            pair = (q0 + j) % 2
                            act.wait_ge(w_used, idx + (u0 + 1))
                            for t in range(TT):
                                op = act.activation(v[t][:, bass.ds(idx * CW, CW)], ps[:, 2 * pair + t, 0:CW], ACT.Gelu)
                            op.then_inc(pair_free, 1)
                        if k:
                            act.wait_ge(y_evac, s["n_group"] + k)
                        phase(12, u0, 4, gelu)
                        u1, q1, g1 = u0 + 12, q0 + 12, s["n_sg"] + 12 * k

                        def group(idx, j, i):
                            for q in range(3):
                                split_next(u1 + q, idx, 6)
                                act.wait_ge(w_used, idx * 6 + (u1 + q + 1))
                                act.wait_ge(pair_free, idx * 3 + (q1 + q + (1 if q == 0 else 0)))
                                act.activation(sg[:, q % 2].rearrange("p (a b) -> p a b", a=2),
                                               ps[:, 2 * (q % 2):2 * (q % 2) + 2, 0:T], ACT.Gelu).then_inc(sg_ready, 1)
                            for q in range(3):
                                split_next(u1 + 3 + q, idx, 6)
                        loop(act, GM_STEPS, 1, group)
                elif s["kind"] == "attn":
                    u0, q0 = s["n_unit"], s["n_inq"]
                    phase(6, u0, 6, copies(u0, q0, ql))
                    phase(2, u0 + 6, 2, copies(u0 + 6, q0 + 6, kvc))
                    AP_.wait(act, "heads", 0)
                    act.activation(qt1[:, 0:4].rearrange("p a b -> p (a b)"), ps[:, 0:2].rearrange("p a b -> p (a b)"),
                                   ACT.Copy)
                    AA.done("heads", act.activation(kt1[:, 0], ps[:, 4], ACT.Copy))
                    exponentials(s["n_item"], Items(1))
                    copy_output(s["n_tr"] + 2)
                    phase(4, u0 + 8, 2)
                elif s["kind"] == "mix":
                    u0, q0, turn = s["n_unit"], s["n_inq"], s["n_mix"]

                    def stage(name, ins_):
                        MA.done(name, ins_)
                        MA.wait(act, name, turn)
                    phase(12, u0, 4, copies(u0, q0, proj))
                    act.wait_ge(mix_full, 160 * (turn + 1) + 32)
                    if turn == 0:
                        act.wait_ge(ang_ready, 1)
                        act.activation(rope2[:].rearrange("p a t f -> p (a t f)"), ang.rearrange("p a t f -> p (a t f)"),
                                       ACT.Sin).then_inc(rope2_ready, 1)
                    stage("cgh", act.activation(cgh, cg_raw, ACT.Copy))
                    MV.wait(act, "absz", turn)
                    steps.link(act.activation(e1[:], e1[:], ACT.Exp))
                    stage("softplus", act.activation(e1[:], e1[:], ACT.Ln, bias=ones[:, 0:1]))
                    MP.wait(act, "sums", turn)
                    sums = [ps[:, b].rearrange("p (t c) -> p t c", t=TT) for b in (5, 6)]
                    act.activation(e1[:], sums[0], ACT.Exp)
                    act.activation(e2[:], sums[0], ACT.Exp, scale=-1.0)
                    act.activation(e3[:], sums[1], ACT.Exp)
                    stage("decays", act.activation(decay, ps[0:64, 7, 0:16], ACT.Exp))
                    MP.wait(act, "qk_t", turn)
                    stage("qt_t", act.activation(qt_t[:].rearrange("p a b -> p (a b)"),
                                                 ps[0:64, 0:2].rearrange("p a b -> p (a b)"), ACT.Copy))
                    stage("silu", act.activation(gg[:], proj[:, :, 2816:3072], ACT.Silu))
                    stage("sig", act.activation(e2[:], proj[:, :, 1792:2048], ACT.Sigmoid))
                    MP.wait(act, "heads", turn)
                    stage("q2", act.activation(q2[:].rearrange("p a b -> p (a b)"),
                                               ps[0:64, 0:4].rearrange("p a b -> p (a b)"), ACT.Copy))
                    exponentials(s["n_item"], Items(2))
                    MV.wait(act, "o_conv", turn)
                    stage("conv", act.activation(om[:, :, 512:768], ctok[:], ACT.Silu))
                    copy_output(s["n_tr"] + 1)
                    phase(4, u0 + 12, 2)

        @block.vector
        def _(dve):
            steps = Steps(dve, vstep)
            dve.memset(st[:], 0.0).then_inc(gb_used, 1)
            dve.sem_inc(wlo_done, FIRST + 1)
            dve.sem_inc(pair_free, FIRST + 1)
            dve.sem_inc(h_ready, FIRST + 1)
            dve.sem_inc(w_used, FIRST)
            dve.sem_inc(mod_used, 2 + 8)
            steps.link(dve.memset(biasrow[:], 0.0))
            dve.sem_inc(bias_used, 1 + 2)

            def mod_unit(s, sec, q):
                cs = conds(s)
                n = 12 * s["i"]
                dve.wait_ge(mraw_full[q % 2], sec * 32 + 16 * (n // 2 + q // 2 + 1))
                if q == 0:
                    dve.wait_ge(bias_full, sec * 16 + 16 * (3 * s["i"] + 1))
                else:
                    dve.wait_ge(mod_used, sec * 4 + (n + q + 2))
                for jj in range(2):
                    for c in cs:
                        v = 2 if s["block"] == 2 else c
                        op = dve.scalar_tensor_tensor(out=acc[:, c], in0=mraw[:, q % 2, jj],
                                                      scalar=svec[:, v, 2 * q + jj:2 * q + jj + 1],
                                                      in1=biasrow[:] if q == jj == 0 else acc[:, c],
                                                      op0=ALU.mult, op1=ALU.add)
                    if jj == 1:
                        op.then_inc(mod_used, 1)
                    elif q == 0:
                        op.then_inc(bias_used, 1)
                        dve.wait_ge(bias_used, sec + (3 * s["i"] + 2))
                    else:
                        steps.link(op)

            def mod_end(s, sec):
                dve.wait_ge(cols_ready, sec + (3 * s["i"] + 1))
                nc_ = len(conds(s))
                dst = modc[:, s["i"] % 2, bass.ds(sec, 1), 0:nc_, :].rearrange("p a c k -> p (a c k)")
                dve.tensor_copy(dst, ps[:, 4, 0:nc_ * KD]).then_inc(mcol_done, 1)

            def split_next(u, i=0, each=0):
                slot = (u + 1) % 2
                dve.wait_ge(whi_done, i * each + (u + 2))
                dve.tensor_tensor(wl[:, slot], wraw[:, slot], wh[:, slot].bitcast(F32), ALU.subtract)\
                    .then_inc(wlo_done, 1)

            def phase(n, u0, per, evac=None, mods=None, marks=0):
                def body(idx, j, i, split=True):
                    if split:
                        split_next(u0 + idx) if isinstance(idx, int) else split_next(u0 + j, i, per)
                    if mods is not None:
                        for sec, q in mods_taken(per, j, i):
                            mod_unit(mods, sec, q)
                    if evac:
                        evac(idx, j, i)
                    if mods is not None and section_done(per, j, i) is not None:
                        mod_end(mods, section_done(per, j, i))
                each = marks + (3 if mods is not None else 0)
                if u0 + n == u_end:
                    loop(dve, n - 1, per, body, steps, each)
                    body(n - 1, (n - 1) % per, 0, False)
                else:
                    loop(dve, n, per, body, steps, each)

            def factors(s):
                b, nc_ = s["i"] % 2, len(conds(s))
                dve.wait_ge(mcol_done, 3 * s["i"] + 3)
                if s["block"] == 1:
                    op = dve.tensor_scalar(prea[:, 0:nc_], modc[:, b, 1, 0:nc_], 1.0, None, ALU.add)
                else:
                    dve.wait_ge(gain_full, 16 * (s["i"] - B2 + 1))
                    op = dve.scalar_tensor_tensor(out=prea[:, 0], in0=modc[:, b, 1, 0], scalar=1.0, in1=gaincol[:],
                                                  op0=ALU.add, op1=ALU.mult)
                op.then_inc(x_mod, 1)
                dve.wait_ge(x_mod, s["i"] + 1)
                if s["block"] == 2:
                    dve.sem_inc(gain_used, 1)

            def split_input(r, c):
                for half in range(2):
                    dve.wait_ge(pre_hi, 2 * r + 1 + half)
                    at = slice(4 * half, 4 * half + 4)
                    dve.tensor_tensor(xl[:, at, c * T:(c + 1) * T], ptmp[:, c, at],
                                      xh[:, at, c * T:(c + 1) * T].bitcast(F32), ALU.subtract).then_inc(pre_ready, 1)

            def prepare_half(s, k, c):
                r = s["n_tr"] + k
                dve.wait_ge(tr_done, r + 1)
                for kc in range(4, 8):
                    last = dve.tensor_scalar(ptmp[:, c, kc], ps[:, kc // 2, (kc % 2) * T:(kc % 2 + 1) * T],
                                             prea[:, c, kc:kc + 1], modc[:, s["i"] % 2, 0, c, kc:kc + 1],
                                             ALU.mult, ALU.add)
                last.then_inc(tr_dve, 1)
                dve.wait_ge(tr_dve, r + 1)
                split_input(r, c)

            def gates(s):
                dve.wait_ge(gate_ps, s["i"] + 1)
                for c in range(len(s["post"])):
                    op = dve.tensor_scalar(gate[:, c], ps[:, 4 + 2 * c:6 + 2 * c].rearrange("p a b -> p (a b)"),
                                           0.5 if s["kind"] == "ffn" else 1.0, None, ALU.mult)
                steps.link(op)

            def take_y(s, streams, bank0, u, first, tiles=None):
                n = TT * len(streams)
                if tiles is None:
                    dve.wait_ge(w_used, u)
                for i in range(n):
                    k, t = divmod(i, TT)
                    c = streams[k]
                    if tiles is not None and i < n - 1:
                        dve.wait_ge(y_tile, tiles + i + 1)
                    elif tiles is not None:
                        dve.wait_ge(w_used, u)
                    b = bank0 + 2 * i
                    if i >= TT:
                        steps.wait(last)
                    steps.link(dve.tensor_tensor(zt[t][:], ps[:, b:b + 2].rearrange("p a b -> p (a b)"), gate[:, c], ALU.mult))
                    if i == n - 1:
                        dve.sem_inc(y_evac, 1)
                    last = steps.mark(dve.scalar_tensor_tensor(
                        out=x[:, c, t], in0=x[:, c, t], scalar=ALPHA if first and s["block"] == 1 else 1.0,
                        in1=zt[t][:], op0=ALU.mult, op1=ALU.add))
                steps.wait(last)

            n_power = [0]

            def layer_norm(s):
                dve.wait_ge(ln_full, 32 * (s["i"] + 1))
                for c in s["post"]:
                    for t in range(TT):
                        for half in range(2):
                            m = steps.mark(dve.bn_stats(st[:, t, half], x[:, c, t, half * 512:(half + 1) * 512]))
                    steps.wait(m)
                    for t in range(TT):
                        m = steps.mark(dve.bn_aggr(mv[:, t], st[:, t, 0:2]))
                    steps.wait(m)
                    dve.tensor_scalar(rstd[:], mv[:, :, 1], LN_EPS, None, ALU.add).then_inc(var_ready, 1)
                    n_power[0] += 1
                    dve.wait_ge(rstd_ready, n_power[0])
                    for t in range(TT):
                        m = steps.mark(dve.tensor_scalar(x[:, c, t], x[:, c, t], mv[:, t, 0:1], rstd[:, t:t + 1],
                                                         ALU.subtract, ALU.mult))
                    for k, op in enumerate((ALU.mult, ALU.add)):
                        for t in range(TT):
                            steps.wait(m - 1)
                            m = steps.mark(dve.tensor_tensor(x[:, c, t], x[:, c, t], lnp[:, k], op))
                    steps.wait(m)
                    dve.sem_inc(x_ready, 1)
                dve.sem_inc(ln_used, 1)

            def root_mean_square(s):
                dve.wait_ge(ssq_ready, TT * (s["i"] - B2 + 1))
                dve.tensor_scalar(rstd[:], rstd[:], 1.0 / D, RMS_EPS, ALU.mult, ALU.add).then_inc(var_ready, 1)
                n_power[0] += 1
                dve.wait_ge(rstd_ready, n_power[0])
                for t in range(TT):
                    m = steps.mark(dve.tensor_scalar(z[:, t], x[:, 0, t], rstd[:, t:t + 1], None, ALU.mult))
                steps.wait(m)
                dve.sem_inc(z_ready, 1)

            def head_squares(src, nh, d, to, buf):
                steps.link(dve.tensor_tensor(buf[:, 0:nh * d], src, src, ALU.mult))
                return steps.mark(dve.reduce_sum(to, buf[:, 0:nh * d].rearrange("p (h d) -> p h d", h=nh), axis=AX.X))

            def head_factors(d):
                steps.link(dve.tensor_scalar(nrm[:], nrm[:], 1.0 / d, RMS_EPS, ALU.mult, ALU.add))
                dve.sem_inc(var_ready, 1)
                n_power[0] += 1
                dve.wait_ge(rstd_ready, n_power[0])

            def norm_heads(a, nh, d, factor, gain):
                a = a.rearrange("p (h d) -> p h d", h=nh)
                steps.link(dve.tensor_tensor(a, a, factor.unsqueeze(2).broadcast_to([P, nh, d]), ALU.mult))
                steps.link(dve.tensor_tensor(a, a, gain.unsqueeze(1).broadcast_to([P, nh, d]), ALU.mult))

            def rotate_heads(a, nh, d, cos, sin, buf):
                half = d // 2
                a = a.rearrange("p (h r d) -> p h r d", h=nh, r=2)
                lo, hi = a[:, :, 0], a[:, :, 1]
                c, s_ = (w.unsqueeze(1).broadcast_to([P, nh, half]) for w in (cos, sin))
                b = buf[:, 0:nh * d].rearrange("p (r h d) -> p r h d", r=2, h=nh)
                dve.tensor_tensor(b[:, 0], lo, s_, ALU.mult)
                steps.link(dve.tensor_tensor(b[:, 1], hi, s_, ALU.mult))
                dve.tensor_tensor(lo, lo, c, ALU.mult)
                steps.link(dve.tensor_tensor(hi, hi, c, ALU.mult))
                dve.tensor_tensor(lo, lo, b[:, 1], ALU.subtract)
                steps.link(dve.tensor_tensor(hi, hi, b[:, 0], ALU.add))

            def softmax_items(n0, items, to):
                def maximum(n):
                    h, t, keys = items[n]
                    dve.wait_ge(s_ps, n0 + n + 1)
                    if items.masked:
                        own = ps[:, n % 2, keys - P:keys]
                        steps.link(dve.tensor_tensor(own, own, causal, ALU.add))
                    steps.link(dve.reduce_max(negm[:, n:n + 1], ps[:, n % 2, 0:keys], axis=AX.X))
                    dve.tensor_scalar(negm[:, n:n + 1], negm[:, n:n + 1], -items.scale, None, ALU.mult)\
                        .then_inc(max_ready, 1)

                for n in range(2):
                    maximum(n)
                for n, (h, t, keys) in enumerate(items):
                    dve.wait_ge(pt_ps, n0 + n + 1)
                    dve.tensor_copy(ht[:, n % 2, 0:keys], ps[:, 2 + n % 2, 0:keys]).then_inc(pt_ready, 1)
                    if n + 2 < len(items):
                        maximum(n + 2)
                    steps.link(dve.reciprocal(den[:, 1, n:n + 1], den[:, 0, n:n + 1]))
                    dve.wait_ge(o_ps, n0 + n + 1)
                    dve.tensor_scalar(to[:, t, h * items.d:(h + 1) * items.d], ps[:, 4 + n % 2, 0:items.d],
                                      den[:, 1, n:n + 1], None, ALU.mult).then_inc(o_taken, 1)

            def copy_output(r):
                dve.wait_ge(tr_done, r + 1)
                dve.tensor_copy(ptmp[:, 0, 4:8].rearrange("p a b -> p (a b)"),
                                ps[:, 2:4].rearrange("p a b -> p (a b)")).then_inc(tr_dve, 1)
                dve.wait_ge(tr_dve, r + 1)
                split_input(r, 0)

            def rope_tables():
                posf, k, r = cg_tok[:, 0:TT], ang[:, 0], ang[:, 1]
                steps.link(dve.tensor_copy(posf, pos[:]))
                a = tm_ang
                for t in range(TT):
                    m = steps.mark(dve.tensor_scalar(a[:, t], freqs, posf[:, t:t + 1], None, ALU.mult))
                steps.wait(m)
                steps.link(dve.tensor_scalar(k, a, 1.0 / (2 * np.pi), ROUND, ALU.mult, ALU.add))
                steps.link(dve.tensor_scalar(k, k, ROUND, None, ALU.subtract))
                for i, part in enumerate(TURN):
                    steps.link(dve.scalar_tensor_tensor(out=r, in0=k, scalar=-part, in1=r if i else a,
                                                        op0=ALU.mult, op1=ALU.add))
                steps.link(dve.tensor_scalar(k, r, np.pi / 2, None, ALU.add))
                steps.link(dve.tensor_scalar(a, k, np.pi, -2 * np.pi, ALU.is_gt, ALU.mult))
                steps.link(dve.tensor_tensor(k, k, a, ALU.add))
                steps.link(dve.tensor_scalar(ang, ang, PI_BELOW, -PI_BELOW, ALU.min, ALU.max))
                dve.sem_inc(ang_ready, 1)
                dve.wait_ge(rope2_ready, 1)

            dve.wait_ge(in_full, 5 * 16)
            dve.wait_ge(svec_ready, 1)

            for q in range(4):
                mod_unit(subs[0], 2, q)
            for half in range(2):
                dve.wait_ge(wst_ps, half + 1)
                dve.tensor_copy(wst[:, 4 * half:4 * half + 4].rearrange("p a b -> p (a b)"), ps[:, half])\
                    .then_inc(wst_ready, 1)
            nc_ = len(conds(subs[0]))
            for sec in range(2):
                dve.wait_ge(first_used, 4 * (sec + 1))
                dve.wait_ge(first_bias, 16)
                dve.tensor_tensor(gate[0:nc_, sec], ps[0:nc_, 4 + 2 * sec:6 + 2 * sec].rearrange("p a b -> p (a b)"),
                                  gate[0:nc_, sec], ALU.add).then_inc(first_rows, 1)
            for sec in range(2):
                dve.wait_ge(cols_ready, sec + 1)
                dve.tensor_copy(modc[:, 0, sec, 0:nc_], ps[:, 2 + sec, 0:nc_ * KD].rearrange("p (k c) -> p c k", c=nc_))\
                    .then_inc(mcol_done, 1)
            dve.sem_inc(cols_ready, 1)
            dve.sem_inc(mcol_done, 1)
            dve.sem_inc(x_ready, len(subs[0]["streams"]))
            dve.wait_ge(whi_done, FIRST + 1)
            dve.tensor_tensor(wl[:, 0], wraw[:, 0], wh[:, 0].bitcast(F32), ALU.subtract).then_inc(wlo_done, 1)
            for s in subs:
                nxt = after(s)
                factors(s)
                if s["block"] == 2:
                    root_mean_square(s)
                for k, c in enumerate(s["streams"]):
                    prepare_half(s, k, c)
                gates(s)
                if s["kind"] == "ffn":
                    W = T * len(s["streams"])
                    m0, u0 = 0, s["n_unit"]
                    for g, n in enumerate(GROUPS):
                        q0, h0 = s["n_inq"] + m0, s["n_h"] + m0
                        g0 = s["n_sg"] + m0

                        def evac(idx, j, i):
                            pair = (q0 + j) % 2
                            dve.wait_ge(sg_ready, idx + (g0 + 1))
                            dve.wait_ge(h_ready, idx + h0)
                            dve.tensor_tensor(ht[:, pair, 0:W], ps[:, 2 * pair + 1, 0:W], sg[:, pair, 0:W], ALU.mult)\
                                .then_inc(pair_free, 1)
                        phase(n, u0, 2 if g else 4, evac, None if g else nxt)
                        phase(n // 2, u0 + n, 2)
                        u0 += n + n // 2
                        take_y(s, s["post"], 0 if W == 2 * T else 4, u0, g == 0,
                               s["n_tile"] + g * (W // P - 1) if g or W == T else None)
                        m0 += n
                elif s["kind"] == "gmlp":
                    for k, c in enumerate(s["streams"]):
                        u0, q0 = s["n_unit"] + 36 * k, s["n_inq"] + 24 * k

                        def stats(idx, j, i):
                            dve.wait_ge(pair_free, idx + (q0 + 2))
                            for t in range(TT):
                                op = dve.bn_stats(st[:, t, bass.ds(idx, 1), :].rearrange("p a b -> p (a b)"),
                                                  v[t][:, bass.ds(idx * CW, CW)])
                            steps.mark(op)
                        phase(12, u0, 4, stats, nxt if k == 0 else None, 4)
                        steps.wait(steps.n)
                        for t in range(TT):
                            m = steps.mark(dve.bn_aggr(mv[:, t], st[:, t]))
                        steps.wait(m)
                        dve.tensor_scalar(rstd[:], mv[:, :, 1], LN_EPS, None, ALU.add).then_inc(var_ready, 1)
                        n_power[0] += 1
                        dve.wait_ge(rstd_ready, n_power[0])
                        u1, q1, g1, h1 = u0 + 12, q0 + 12, s["n_sg"] + 12 * k, s["n_h"] + 12 * k

                        def group(idx, j, i):
                            dve.wait_ge(w_used, idx * 6 + (u1 - 3))
                            dve.wait_ge(gb_full, idx * 32 + 32 * (GM_STEPS * k + 1))
                            for t in range(TT):
                                m = steps.mark(dve.tensor_scalar(vg[:, t], v[t][:, bass.ds(idx * GM_GROUP, GM_GROUP)],
                                                                 mv[:, t, 0:1], rstd[:, t:t + 1],
                                                                 ALU.subtract, ALU.mult))
                            for b, op in enumerate((ALU.mult, ALU.add)):
                                steps.wait(m)
                                for t in range(TT):
                                    m = steps.mark(dve.tensor_tensor(vg[:, t], vg[:, t], gb[:, b], op))
                            steps.wait(m)
                            dve.sem_inc(gb_used, 1)
                            dve.sem_inc(vg_ready, 1)
                            for q in range(3):
                                split_next(u1 + q, idx, 6)
                                dve.wait_ge(sg_ready, idx * 3 + (g1 + q + 1))
                                dve.wait_ge(h_ready, idx * 3 + (h1 + q + (1 if q == 0 else 0)))
                                dve.tensor_tensor(ht[:, q % 2].rearrange("p (a b) -> p a b", a=2),
                                                  ps[:, 2 * (q % 2):2 * (q % 2) + 2, T:2 * T],
                                                  sg[:, q % 2].rearrange("p (a b) -> p a b", a=2), ALU.mult)\
                                    .then_inc(pair_free, 1)
                            for q in range(3):
                                split_next(u1 + 3 + q, idx, 6)
                        loop(dve, GM_STEPS, 1, group, steps, 6)
                        dve.wait_ge(y_closed, k + 1)
                        take_y(s, (c,), 4, u0 + 36, True)
                elif s["kind"] == "attn":
                    u0, q0 = s["n_unit"], s["n_inq"]
                    steps.link(dve.memset(nrm[:], 1.0))
                    phase(6, u0, 6, None, nxt)
                    phase(2, u0 + 6, 2)
                    dve.wait_ge(pair_free, q0 + 9)
                    dve.wait_ge(att_full, 64)
                    for t in range(TT):
                        head_squares(ql[:, t, 0:1280], HEADS + KV_HEADS, HD, nrm[:, t, 0:10], tm1[:, 0])
                        m = head_squares(kvc[:, t, 0:256], KV_HEADS, HD, nrm[:, t, 10:12], tm1[:, 1])
                        steps.wait(m)
                    head_factors(HD)
                    for t in range(TT):
                        norm_heads(ql[:, t, 0:1024], HEADS, HD, nrm[:, t, 0:8], hgain[:, 0])
                        norm_heads(ql[:, t, 1024:1280], KV_HEADS, HD, nrm[:, t, 8:10], hgain[:, 1])
                        norm_heads(kvc[:, t, 0:256], KV_HEADS, HD, nrm[:, t, 10:12], hgain[:, 1])
                        rotate_heads(ql[:, t, 0:1280], HEADS + KV_HEADS, HD, rope[:, t, 0], rope[:, t, 1], tm1[:, t])
                    AV.done("shaped", dve.memset(st[:, 0, 0], 0.0))
                    AP_.wait(dve, "heads", 0)
                    dve.tensor_copy(qt1[:, 4:8].rearrange("p a b -> p (a b)"), ps[:, 2:4].rearrange("p a b -> p (a b)"))
                    AV.done("heads", dve.tensor_copy(kt1[:, 1], ps[:, 5]))
                    softmax_items(s["n_item"], Items(1), z)
                    copy_output(s["n_tr"] + 2)
                    phase(4, u0 + 8, 2)
                    take_y(s, (0,), 4, u0 + 12, True, s["n_tile"])
                elif s["kind"] == "mix":
                    u0, q0, turn = s["n_unit"], s["n_inq"], s["n_mix"]

                    def stage(name, ins_):
                        MV.done(name, ins_)
                        MV.wait(dve, name, turn)
                    phase(12, u0, 4, None, nxt)
                    dve.wait_ge(pair_free, q0 + 13)
                    dve.wait_ge(mix_full, 160 * (turn + 1) + 32)
                    MG.wait(dve, "masks", turn)
                    if turn == 0:
                        rope_tables()
                    MA.wait(dve, "cgh", turn)
                    stage("cgl", dve.tensor_tensor(cgl, cg_raw, cgh.bitcast(F32), ALU.subtract))
                    MP.wait(dve, "cg", turn)
                    dve.tensor_copy(cg_tok, ps[:, 5, 0:32])
                    stage("cgt", dve.memset(cg_t[:], 1.0))
                    MP.wait(dve, "cg_t", turn)
                    stage("cg_t", dve.tensor_copy(cg_t[0:16], ps[0:16, 6, 0:T]))
                    MP.wait(dve, "z", turn)
                    zg = ps[:, 5].rearrange("p (t c) -> p t c", t=TT)
                    dve.tensor_scalar(e1[:], zg, 0.0, None, ALU.max)
                    steps.link(dve.tensor_scalar(e2[:], zg, 0.0, None, ALU.min))
                    stage("absz", dve.tensor_tensor(e1[:], e2[:], e1[:], ALU.subtract))
                    MA.wait(dve, "softplus", turn)
                    steps.link(dve.tensor_tensor(gg[:], e2[:], e1[:], ALU.subtract))
                    stage("g", dve.tensor_scalar(gg[:], gg[:], 1.0 / 16.0, None, ALU.mult))
                    MA.wait(dve, "decays", turn)
                    c_q, c_k = proj[:, :, 2048:2304], proj[:, :, 2304:2560]
                    dve.scalar_tensor_tensor(out=e1[:], in0=c_q, scalar=G_D ** -0.5, in1=e1[:], op0=ALU.mult, op1=ALU.mult)
                    dve.tensor_tensor(kt[:], c_k, e2[:], ALU.mult)
                    for j in range(2):
                        op = dve.scalar_tensor_tensor(out=ke[:, j], in0=c_k, scalar=tri[:, 64 * j + 63:64 * j + 64],
                                                      in1=e3[:], op0=ALU.mult, op1=ALU.mult)
                    stage("qk", op)
                    steps.link(dve.memset(qeo[:], 0.0))
                    MP.wait(dve, "qk_t", turn)
                    MA.wait(dve, "qt_t", turn)
                    for h in range(G_HEADS):
                        src = qt_t[:, h].rearrange("p (t j d) -> p t j d", t=TT, j=2)
                        dst = qeo[:, :, h].rearrange("p e (t j d) -> p e t j d", t=TT, j=2)
                        for j in range(2):
                            dve.tensor_copy(dst[:, j, :, j], src[:, :, j])
                    stage("kt_t", dve.tensor_copy(kt_t[:].rearrange("p a b -> p (a b)"),
                                                  ps[0:64, 2:4].rearrange("p a b -> p (a b)")))
                    MP.wait(dve, "scores", turn)
                    dve.tensor_tensor(sc_t[:], ps[:, 4:6].rearrange("p a (b c) -> p (a b) c", c=P),
                                      tri.unsqueeze(1).broadcast_to([P, TT * G_HEADS, P]), ALU.mult)
                    steps.link(dve.tensor_copy(kvs[:].rearrange("p a b c -> p (a b c)"),
                                               ps[0:64, 6:8].rearrange("p a b -> p (a b)")))
                    for n in (1, 2):
                        for h in range(G_HEADS):
                            before = kvs[:, h, 0] if n == 1 else sts[:, h, 1]
                            op = dve.scalar_tensor_tensor(out=sts[:, h, n], in0=before, scalar=decay[:, h * 4 + n:h * 4 + n + 1],
                                                          in1=kvs[:, h, n], op0=ALU.mult, op1=ALU.add)
                        steps.link(op)
                    stage("states", dve.memset(nrm[:], 1.0))
                    MP.wait(dve, "o", turn)
                    o_c = om[:, :, 768:1024]
                    steps.link(dve.tensor_copy(o_c, ps[:, 0:2, 0:256]))
                    for t in range(TT):
                        m = head_squares(om[:, t, 768:1024], G_HEADS, G_D, nrm[:, t, 0:G_HEADS], tm2[:, t])
                    steps.wait(m)
                    head_factors(G_D)
                    for t in range(TT):
                        norm_heads(om[:, t, 768:1024], G_HEADS, G_D, nrm[:, t, 0:G_HEADS], out_norm)
                    MA.wait(dve, "silu", turn)
                    stage("oc", dve.tensor_tensor(o_c, o_c, gg[:], ALU.mult))
                    MA.wait(dve, "sig", turn)
                    stage("h", dve.tensor_tensor(e2[:], e2[:], proj[:, :, 1536:1792], ALU.mult))
                    for t in range(TT):
                        m = head_squares(proj[:, t, 0:1024], 2 * M_HEADS, M_HD, nrm[:, t], tm2[:, t])
                    steps.wait(m)
                    head_factors(M_HD)
                    for t in range(TT):
                        for g in range(2):
                            norm_heads(proj[:, t, g * 512:(g + 1) * 512], M_HEADS, M_HD, nrm[:, t, g * 8:(g + 1) * 8],
                                       hgain[:, g, 0:M_HD])
                        rotate_heads(proj[:, t, 0:1024], 2 * M_HEADS, M_HD, rope2[:, 0, t], rope2[:, 1, t], tm2[:, t])
                    stage("shaped", dve.memset(ch_t[:, :, 0:CONV_K - 1], 0.0))
                    MP.wait(dve, "heads", turn)
                    stage("k2", dve.tensor_copy(k2[:].rearrange("p a b -> p (a b)"),
                                                ps[0:64, 4:8].rearrange("p a b -> p (a b)")))
                    MP.wait(dve, "h_t", turn)
                    dve.tensor_copy(ch_t[:, :, CONV_K - 1:CONV_K - 1 + T], ps[:, 6].rearrange("p (a b) -> p a b", a=2))
                    stage("ch_t", dve.tensor_copy(cw_t[:].rearrange("p a b -> p (a b)"), ps[:, 7, 0:64]))
                    for tap in range(CONV_K):
                        for cc in range(2):
                            w, b = cw_t[:, cc, tap:tap + 1], cw_t[:, cc, CONV_K:CONV_K + 1]
                            src = ch_t[:, cc, tap:tap + T]
                            if tap == 0:
                                m = steps.mark(dve.tensor_scalar(cacc[:, cc], src, w, b, ALU.mult, ALU.add))
                            else:
                                steps.wait(m - 1)
                                op = dve.scalar_tensor_tensor(out=cacc[:, cc], in0=src, scalar=w, in1=cacc[:, cc],
                                                              op0=ALU.mult, op1=ALU.add)
                                m = steps.mark(op)
                    steps.wait(m)
                    dve.sem_inc(MV.sem, 1)
                    MV.skip("taps")
                    softmax_items(s["n_item"], Items(2), om)
                    MP.wait(dve, "conv", turn)
                    steps.link(dve.tensor_copy(ctok[:].rearrange("p a b -> p (a b)"), ps[:, 6]))
                    grp = ctok[:].rearrange("p t (g c) -> p (t g) c", c=64)
                    for g in range(8):
                        m = steps.mark(dve.bn_stats(hst[:, g], grp[:, g]))
                    steps.wait(m)
                    for g in range(8):
                        m = steps.mark(dve.bn_aggr(hmv[:, g], hst[:, g]))
                    steps.wait(m)
                    steps.link(dve.tensor_scalar(hrs, hmv[:, :, 1], RMS_EPS, None, ALU.add))
                    dve.sem_inc(var_ready, 1)
                    n_power[0] += 1
                    steps.link(dve.tensor_tensor(grp, grp, hmv[:, :, 0:1].broadcast_to([P, 8, 64]), ALU.subtract))
                    dve.wait_ge(rstd_ready, n_power[0])
                    stage("stats", dve.tensor_tensor(grp, grp, hrs.unsqueeze(2).broadcast_to([P, 8, 64]), ALU.mult))
                    for j, op in enumerate((ALU.mult, ALU.add)):
                        last = dve.tensor_tensor(ctok[:], ctok[:], conv_norm[:, j].unsqueeze(1).broadcast_to([P, TT, 256]), op)
                        if j == 0:
                            steps.link(last)
                    stage("o_conv", last)
                    copy_output(s["n_tr"] + 1)
                    phase(4, u0 + 12, 2)
                    take_y(s, (0,), 4, u0 + 16, True, s["n_tile"])
                if s["block"] == 1:
                    layer_norm(s)
                else:
                    dve.sem_inc(x_ready, 1)

        @block.tensor
        def _(pe):
            def parts(w_hi, w_lo, x_hi, x_lo):
                return (w_hi, x_hi), (w_lo, x_hi), (w_hi, x_lo)

            def columns(s, sec):
                pe.wait_ge(mod_used, sec * 4 + (12 * s["i"] + 6))
                for c in conds(s):
                    for k in range(KD):
                        m = pe.matmul(ps[:, 4, c * KD + k:c * KD + k + 1], acc[:, c, k * P:(k + 1) * P],
                                      ones[:, 0:1], start=True, stop=True)
                m.then_inc(cols_ready, 1)

            def gate_rows(s):
                pe.wait_ge(mcol_done, 3 * s["i"] + 3)
                pe.wait_ge(y_evac, s["n_group"])
                for c in range(len(s["post"])):
                    for half in range(2):
                        m = pe.matmul(ps[:, 4 + 2 * c + half], ones[:], acc[:, c, half * 512:(half + 1) * 512],
                                      start=True, stop=True)
                m.then_inc(gate_ps, 1)

            def transposes(s):
                for k, c in enumerate(s["streams"]):
                    r = s["n_tr"] + k
                    pe.wait_ge(x_ready, s["n_pre"] + k + 1)
                    if s["block"] == 2:
                        pe.wait_ge(z_ready, s["i"] - B2 + 1)
                    pe.wait_ge(tr_act, r)
                    pe.wait_ge(tr_dve, r)
                    src = x[:, c] if s["block"] == 1 else z
                    transpose_stream(src)

            def transpose_stream(src):
                for t in range(TT):
                    for kc in range(KD):
                        off = (kc % 2) * T + t * P
                        m = pe.transpose(ps[:, kc // 2, off:off + P], src[:, t, kc * P:(kc + 1) * P], ident[:])
                m.then_inc(tr_done, 1)

            def features(slot, bank, r, tokens, width):
                for k in range(KD):
                    at = slice(k * CW + r * P, k * CW + (r + 1) * P)
                    for p, (a, b) in enumerate(parts(wh[:, slot, at], wl[:, slot, at], xh[:, k, tokens], xl[:, k, tokens])):
                        m = pe.matmul(ps[:, bank, 0:width], a, b, start=k == p == 0, stop=k == KD - 1 and p == 2)
                return m

            def features_phase(n, u0, q0, width, per, mods=None):
                def body(idx, j, i):
                    slot, pair = (u0 + j) % 2, (q0 + j) % 2
                    pe.wait_ge(wlo_done, idx + (u0 + 2))
                    pe.wait_ge(pair_free, idx + q0)
                    for r in range(2):
                        m = features(slot, 2 * pair + r, r, slice(0, width), width)
                    m.then_inc(w_used, 1)
                    if mods is not None and section_done(per, j, i) is not None:
                        columns(mods, section_done(per, j, i))
                loop(pe, n, per, body)

            def tokens_phase(n, u0, q0, c, per, mods=None):
                def body(idx, j, i):
                    slot, pair = (u0 + j) % 2, (q0 + j) % 2
                    pe.wait_ge(wlo_done, idx + (u0 + 2))
                    pe.wait_ge(pair_free, idx + q0)
                    for t in range(TT):
                        at = slice(c * T + t * P, c * T + (t + 1) * P)
                        for k in range(KD):
                            w = slice(k * CW, (k + 1) * CW)
                            for p, (b, a) in enumerate(parts(wh[:, slot, w], wl[:, slot, w], xh[:, k, at], xl[:, k, at])):
                                m = pe.matmul(ps[:, 2 * pair + t, 0:CW], a, b, start=k == p == 0,
                                              stop=k == KD - 1 and p == 2)
                    m.then_inc(w_used, 1)
                    if mods is not None and section_done(per, j, i) is not None:
                        columns(mods, section_done(per, j, i))
                loop(pe, n, per, body)

            def out_unit(u, count, width, bank0, chunk0, ready, start=False, stop=False, halves=None):
                slot = u % 2
                pe.wait_ge(wlo_done, count + 2)
                ready()
                for t in range(width // P):
                    for kk in range(2):
                        at = slice((chunk0 + kk) * width + t * P, (chunk0 + kk) * width + (t + 1) * P)
                        x_hi, x_lo = halves(chunk0 + kk, t) if halves else (hh[:, at], hl[:, at])
                        for half in range(2):
                            w = slice(kk * D + half * 512, kk * D + (half + 1) * 512)
                            for p, (b, a) in enumerate(parts(wh[:, slot, w], wl[:, slot, w], x_hi, x_lo)):
                                m = pe.matmul(ps[:, bank0 + 2 * t + half], a, b, start=start and kk == p == 0,
                                              stop=stop and kk == 1 and p == 2, skip_group_check=not start and not stop)
                    if stop and t < width // P - 1:
                        m.then_inc(y_tile, 1)
                m.then_inc(w_used, 1)

            def add_zero(banks, start):
                for b in banks:
                    for at in range(0, 512, P):
                        m = pe.matmul(ps[:, b, at:at + P], zeros[:], zeros[:], start=start and at == 0, stop=not start,
                                      skip_group_check=True)
                return m

            def out_phase(n, u0, width, bank0, ready, halves=None):
                for i in range(n):
                    out_unit(u0 + i, u0 + i, width, bank0, 2 * i, lambda: ready(i), i == 0, i == n - 1, halves)

            def input_halves(chunk, t):
                return tuple(w[:, chunk, t * P:(t + 1) * P] for w in (xh, xl))

            def attention(n0, items, q, k, v):
                def scores(n):
                    h, t, keys = items[n]
                    if n >= 2:
                        pe.wait_ge(p_ready, n0 + n - 1)
                    pe.matmul(ps[:, n % 2, 0:keys], q[:, h, t * P:(t + 1) * P], k(h)[:, 0:keys], start=True, stop=True)\
                        .then_inc(s_ps, 1)

                for n in range(2):
                    scores(n)
                for n, (h, t, keys) in enumerate(items):
                    pe.wait_ge(p_ready, n0 + n + 1)
                    if n >= 2:
                        pe.wait_ge(pt_ready, n0 + n - 1)
                    for a in range(0, keys, P):
                        m = pe.transpose(ps[:, 2 + n % 2, a:a + P], sg[:, n % 2, a:a + P], ident[:])
                    m.then_inc(pt_ps, 1)
                    if n + 2 < len(items):
                        scores(n + 2)
                    pe.wait_ge(pt_ready, n0 + n + 1)
                    if n >= 2:
                        pe.wait_ge(o_taken, n0 + n - 1)
                    for c in range(keys // P):
                        m = pe.matmul(ps[:, 4 + n % 2, 0:items.d], ht[:, n % 2, c * P:(c + 1) * P], v(h, c),
                                      start=c == 0, stop=c == keys // P - 1)
                    m.then_inc(o_ps, 1)

            pe.wait_ge(ident_ready, 2)
            pe.wait_ge(ws_full, 16)
            for g in range(SG_GROUPS):
                m = pe.transpose(ps[:, g // 4, (g % 4) * P:(g % 4 + 1) * P],
                                 ht[:, g // 4, (g % 4) * P:(g % 4 + 1) * P], ident[:])
                if g % 4 == 3:
                    m.then_inc(wst_ps, 1)
            pe.wait_ge(svec_ready, 1)
            cs = slice(2, 3) if subs[0]["block"] == 2 else slice(0, 2)
            nc_ = len(conds(subs[0]))
            for n in range(8):
                sec, q = divmod(n, 4)
                pe.wait_ge(first_full[n % 6], 16 * (n // 6 + 1))
                for half in range(2):
                    for jj in range(2):
                        m = pe.matmul(ps[0:nc_, 4 + 2 * sec + half], svec[:, cs, 2 * q + jj],
                                      first_w[:, n % 6, jj, half * 512:(half + 1) * 512],
                                      start=q == jj == 0, stop=q == 3 and jj == 1)
                m.then_inc(first_used, 1)
            for sec in range(2):
                pe.wait_ge(first_rows, sec + 1)
                for kc in range(KD):
                    m = pe.transpose(ps[:, 2 + sec, nc_ * kc:nc_ * (kc + 1)], gate[0:nc_, sec, kc * P:(kc + 1) * P],
                                     ident[0:nc_, 0:nc_])
                m.then_inc(cols_ready, 1)
            pe.wait_ge(mod_used, 14)
            pe.wait_ge(wst_ready, 2)
            for s in subs:
                nxt = after(s)
                gate_rows(s)
                transposes(s)
                pe.wait_ge(pre_ready, 2 * (s["n_tr"] + len(s["streams"])))
                if s["kind"] == "ffn":
                    W = T * len(s["streams"])
                    both = W == 2 * T
                    m0, u0 = 0, s["n_unit"]
                    for g, n in enumerate(GROUPS):
                        if both:
                            pe.wait_ge(y_evac, s["n_group"] + g)
                        features_phase(n, u0, s["n_inq"] + m0, W, 2 if g else 4, None if g else nxt)
                        pe.wait_ge(pair_free, s["n_inq"] + m0 + n + 1)
                        pe.wait_ge(y_evac, s["n_group"] + g)
                        if g == 0 and nxt:
                            pe.wait_ge(mcol_done, 3 * s["i"] + 6)
                        out_phase(n // 2, u0 + n, W, 0 if both else 4,
                                  lambda i: pe.wait_ge(h_ready, s["n_h"] + m0 + 2 * i + 3))
                        m0 += n
                        u0 += n + n // 2
                elif s["kind"] == "gmlp":
                    for k, c in enumerate(s["streams"]):
                        u0, q0 = s["n_unit"] + 36 * k, s["n_inq"] + 24 * k
                        tokens_phase(12, u0, q0, c, 4, nxt if k == 0 else None)
                        u1, q1, h1 = u0 + 12, q0 + 12, s["n_h"] + 12 * k
                        pe.wait_ge(y_evac, s["n_group"] + k)
                        pe.wait_ge(bs_full, 16)
                        if k == 0 and nxt:
                            pe.wait_ge(mcol_done, 3 * s["i"] + 6)
                        add_zero(range(4, 8), True)

                        def group(idx, j, i):
                            for q in range(3):
                                slot, pair = (u1 + q) % 2, q % 2
                                pe.wait_ge(wlo_done, idx * 6 + (u1 + q + 2))
                                pe.wait_ge(pair_free, idx * 3 + (q1 + q + (1 if q == 0 else 0)))
                                if q == 0:
                                    pe.wait_ge(vg_ready, idx + (GM_STEPS * k + 1))
                                for r in range(2):
                                    features(slot, 2 * pair + r, r, slice(c * T, (c + 1) * T), T)
                                for r in range(2):
                                    m = 2 * q + r
                                    g = idx * 2 + m // 3
                                    for t in range(TT):
                                        to = ps[:, 2 * pair + r, T + t * P:T + (t + 1) * P]
                                        pe.matmul(to, vg[:, t, m * P:(m + 1) * P],
                                                  wst[:, bass.ds(g, 1), :].rearrange("p a b -> p (a b)"),
                                                  start=True, stop=False)
                                        last = pe.matmul(to, ones[0:1, :], bsrow[:, bass.ds(g * P, P)],
                                                         start=False, stop=True)
                                last.then_inc(w_used, 1)
                            for q in range(3):
                                out_unit(u1 + 3 + q, idx * 6 + (u1 + 3 + q), T, 4, 2 * q,
                                         lambda: pe.wait_ge(h_ready, idx * 3 + (h1 + q + 2)))
                        loop(pe, GM_STEPS, 1, group)
                        add_zero(range(4, 8), False).then_inc(y_closed, 1)
                elif s["kind"] == "attn":
                    u0, q0 = s["n_unit"], s["n_inq"]
                    tokens_phase(6, u0, q0, 0, 6, nxt)
                    tokens_phase(2, u0 + 6, q0 + 6, 1, 2)
                    AV.wait(pe, "shaped", 0)
                    pe.wait_ge(pair_free, q0 + 9)
                    for n in range(HEADS * TT):
                        h, t = divmod(n, TT)
                        pe.transpose(ps[:, n // 4, (n % 4) * P:(n % 4 + 1) * P], ql[:, t, h * HD:(h + 1) * HD], ident[:])
                    for h in range(KV_HEADS):
                        for t in range(2 * TT):
                            src = kvc[:, t] if t < TT else ql[:, t - TT, HEADS * HD:]
                            m = pe.transpose(ps[:, 4 + h, t * P:(t + 1) * P], src[:, h * HD:(h + 1) * HD], ident[:])
                    AP_.done("heads", m)
                    AA.wait(pe, "heads", 0)
                    AV.wait(pe, "heads", 0)

                    def values(h, c):
                        at = (h // (HEADS // KV_HEADS) + KV_HEADS) * HD
                        src = kvc[:, c] if c < TT else ql[:, c - TT, HEADS * HD:]
                        return src[:, at:at + HD]
                    items = Items(1)
                    attention(s["n_item"], items, qt1, lambda h: kt1[:, h // (HEADS // KV_HEADS)], values)
                    pe.wait_ge(o_taken, s["n_item"] + len(items))
                    transpose_stream(z)
                    pe.wait_ge(pre_ready, 2 * (s["n_tr"] + 3))
                    out_phase(4, u0 + 8, T, 4, lambda i: None, input_halves)
                elif s["kind"] == "mix":
                    u0, q0, turn = s["n_unit"], s["n_inq"], s["n_mix"]
                    tokens_phase(12, u0, q0, 0, 4, nxt)
                    MV.wait(pe, "cgl", turn)
                    for t in range(TT):
                        at = slice(t * P, (t + 1) * P)
                        for k in range(KD):
                            w = slice(k * 16, (k + 1) * 16)
                            for p, (b, a) in enumerate(parts(cgh[:, w], cgl[:, w], xh[:, k, at], xl[:, k, at])):
                                m = pe.matmul(ps[:, 5, t * 16:(t + 1) * 16], a, b, start=k == p == 0,
                                              stop=k == KD - 1 and p == 2)
                    MP.done("cg", m)
                    MV.wait(pe, "cgt", turn)
                    for t in range(TT):
                        m = pe.transpose(ps[0:16, 6, t * P:(t + 1) * P], cg_tok[:, t * 16:(t + 1) * 16], ident[:])
                    MP.done("cg_t", m)
                    MV.wait(pe, "cg_t", turn)
                    for t in range(TT):
                        m = pe.matmul(ps[:, 5, t * T:(t + 1) * T], cg_t[0:17, t * P:(t + 1) * P], gate_raw[0:17],
                                      start=True, stop=True)
                    MP.done("z", m)
                    MV.wait(pe, "g", turn)
                    for t in range(TT):
                        for bank, mask in ((5, tri), (6, suf)):
                            pe.matmul(ps[:, bank, t * T:(t + 1) * T], mask, gg[:, t], start=True, stop=True)
                        for h in range(G_HEADS):
                            at = (h * TT + t) * 2
                            m = pe.matmul(ps[0:64, 7, at:at + 2], gg[:, t, h * G_D:(h + 1) * G_D], tri[:, 63:P:64],
                                          start=True, stop=True)
                    MP.done("sums", m)
                    MV.wait(pe, "qk", turn)
                    for bank, src in ((0, e1), (2, kt)):
                        for h in range(G_HEADS):
                            for t in range(TT):
                                at = (h % 2) * T + t * P
                                m = pe.transpose(ps[0:64, bank + h // 2, at:at + P], src[:, t, h * G_D:(h + 1) * G_D], ident[:])
                    MP.done("qk_t", m)
                    MA.wait(pe, "qt_t", turn)
                    MV.wait(pe, "kt_t", turn)
                    for t in range(TT):
                        for h in range(G_HEADS):
                            pe.matmul(ps[:, 4 + t, h * P:(h + 1) * P], kt_t[:, h, t * P:(t + 1) * P],
                                      qt_t[:, h, t * P:(t + 1) * P], start=True, stop=True)
                            cv = proj[:, t, 2560 + h * G_D:2560 + (h + 1) * G_D]
                            for j in range(2):
                                at = (h % 2) * T + (2 * t + j) * G_D
                                m = pe.matmul(ps[0:64, 6 + h // 2, at:at + G_D], ke[:, j, t, h * G_D:(h + 1) * G_D], cv,
                                              start=True, stop=True)
                    MP.done("scores", m)
                    MV.wait(pe, "states", turn)
                    for t in range(TT):
                        for h in range(G_HEADS):
                            to = ps[:, t, h * G_D:(h + 1) * G_D]
                            pe.matmul(to, sc_t[:, t * G_HEADS + h], proj[:, t, 2560 + h * G_D:2560 + (h + 1) * G_D],
                                      start=True, stop=False)
                            for j in range(0 if t else 1, 2):
                                n = 2 * t + j
                                state = kvs[:, h, 0] if n == 1 else sts[:, h, n - 1]
                                m = pe.matmul(to, qeo[:, j, h, t * P:(t + 1) * P], state, start=False, stop=j == 1)
                    MP.done("o", m)
                    MV.wait(pe, "shaped", turn)
                    for g in range(2):
                        for h in range(M_HEADS):
                            for t in range(TT):
                                at = (h % 2) * T + t * P
                                src = proj[:, t, g * 512 + h * M_HD:g * 512 + (h + 1) * M_HD]
                                m = pe.transpose(ps[0:64, 4 * g + h // 2, at:at + P], src, ident[:])
                    MP.done("heads", m)
                    MV.wait(pe, "k2", turn)
                    MA.wait(pe, "q2", turn)
                    for cc in range(2):
                        for t in range(TT):
                            pe.transpose(ps[:, 6, cc * T + t * P:cc * T + (t + 1) * P], e2[:, t, cc * P:(cc + 1) * P], ident[:])
                        m = pe.transpose(ps[:, 7, cc * 32:(cc + 1) * 32], conv_raw[:, cc * P:(cc + 1) * P], ident[0:32, 0:32])
                    MP.done("h_t", m)
                    items = Items(2)
                    attention(s["n_item"], items, q2, lambda h: k2[:, h],
                              lambda h, c: proj[:, c, 1024 + h * M_HD:1024 + (h + 1) * M_HD])
                    MV.wait(pe, "taps", turn)
                    for cc in range(2):
                        for t in range(TT):
                            m = pe.transpose(ps[:, 6, t * T + cc * P:t * T + (cc + 1) * P], cacc[:, cc, t * P:(t + 1) * P], ident[:])
                    MP.done("conv", m)
                    pe.wait_ge(o_taken, s["n_item"] + len(items))
                    MA.wait(pe, "conv", turn)
                    transpose_stream(om)
                    pe.wait_ge(pre_ready, 2 * (s["n_tr"] + 2))
                    out_phase(4, u0 + 12, T, 4, lambda i: None, input_halves)


_INS = ("x", "c", "ctx", "c_ctx", "w_mod", "b_mod", "ln_g", "ln_b", "ffn_w_in", "ffn_w_out", "gmlp_w_in", "gmlp_ln_g",
        "gmlp_ln_b", "gmlp_w_s", "gmlp_b_s", "gmlp_w_out", "attn_w_qkv", "attn_q_norm", "attn_k_norm", "attn_w_o",
        "c_2", "positions_2", "ada_w_2", "ada_b_2", "ffn1_norm_2", "ffn1_w_in_2", "ffn1_w_out_2", "mix_norm_2",
        "mix_w_in_2", "q_norm_2", "k_norm_2", "conv_w_2", "conv_b_2", "conv_norm_g_2", "conv_norm_b_2",
        "gla_gate_w_2", "gla_gate_b_2", "gla_out_norm_2", "mix_w_out_2", "ffn2_norm_2", "ffn2_w_in_2", "ffn2_w_out_2")


def rope_constants():
    quarter = HD // 4
    freqs = (10000.0 ** (-np.arange(quarter) / quarter)).astype(np.float32)
    t = np.arange(T)
    ang = np.concatenate([(t // 64).astype(np.float32)[:, None] * freqs, (t % 64).astype(np.float32)[:, None] * freqs], -1)
    inv = np.float32(1.0) / (10000.0 ** (np.arange(0, M_HD, 2) / M_HD)).astype(np.float32)
    return (np.stack([np.cos(ang), np.sin(ang)]).astype(np.float32), inv.astype(np.float32)[None])


def kernel(**inputs):
    import concourse.bacc as bacc
    from concourse.bass_utils import run_bass_kernel_spmd

    nc = bacc.Bacc("TRN2", target_bir_lowering=False, num_devices=1)
    arrays = {n: np.ascontiguousarray(inputs[n]) for n in _INS}
    arrays["rope_1"], arrays["rope_freqs_2"] = rope_constants()
    ins = {n: nc.dram_tensor(f"in_{n}", a.shape, mybir.dt.from_np(a.dtype), kind="ExternalInput").ap()
           for n, a in arrays.items()}
    out = nc.dram_tensor("out_0", (1, T, D), F32, kind="ExternalOutput").ap()
    program(nc, ins, out, plan())
    r = run_bass_kernel_spmd(nc, [{f"in_{n}": a for n, a in arrays.items()}], core_ids=[0])
    return r.results[0]["out_0"]
```

```python
from contextlib import ExitStack

import numpy as np
import concourse.bass as bass
from concourse import mybir

P = 128
B2 = 6
F32 = mybir.dt.float32
F32R = mybir.dt.float32r
I32 = mybir.dt.int32
ALU = mybir.AluOpType
ACT = mybir.ActivationFunctionType
AX = mybir.AxisListType

D = 1024
KD = D // P
T = 256
TT = T // P
DEPTH = 2
D_FF = 2816
KF = D_FF // P
GROUPS = (12, 10)
GM_HALF = 3072
GM_GROUP = 768
GM_STEPS = GM_HALF // GM_GROUP
SG_GROUPS = 8
HEADS, KV_HEADS, HD = 8, 2, 128
QKV = (HEADS + 2 * KV_HEADS) * HD
M_HEADS, M_HD = 8, 64
G_HEADS, G_D = 4, 64
IN_W = 3088
CONV_K = 31
ALPHA = (2.0 * DEPTH) ** 0.25
LN_EPS, RMS_EPS = 1e-5, 1e-6
NEG = -1e30
FIRST = 2
ROUND = 1.5 * 2.0 ** 23
TURN = (6.28125, 0.0019350051879882812, 3.019915981956753e-07)
PI_BELOW = 3.1415925
CW = 256


def plan():
    subs = []
    for l in range(DEPTH):
        both = (0, 1)
        last = l == DEPTH - 1
        mixer = "attn" if l % 2 else "gmlp"
        subs.append(dict(block=1, layer=l, kind="ffn", part=0, streams=both, post=both))
        subs.append(dict(block=1, layer=l, kind=mixer, part=1, streams=both, post=(0,) if last else both))
        subs.append(dict(block=1, layer=l, kind="ffn", part=2, streams=(0,) if last else both,
                         post=(0,) if last else both))
    for l in range(DEPTH):
        for part, kind in enumerate(("ffn", "mix", "ffn")):
            subs.append(dict(block=2, layer=l, kind=kind, part=part, streams=(0,), post=(0,)))
    n = dict(unit=FIRST, inq=FIRST, h=FIRST, sg=0, group=0, pre=0, tr=0, item=0, mix=0, tile=0)
    for i, s in enumerate(subs):
        s["i"] = i
        s.update({"n_" + k: v for k, v in n.items()})
        ns = len(s["streams"])
        n["pre"] += ns
        n["tr"] += ns + (s["kind"] in ("attn", "mix"))
        if s["kind"] == "ffn":
            n["unit"] += KF + KF // 2
            n["inq"] += KF
            n["h"] += KF
            n["sg"] += KF
            n["group"] += len(GROUPS)
            n["tile"] += len(GROUPS) * (TT * ns - 1)
        elif s["kind"] == "gmlp":
            n["unit"] += ns * 36
            n["inq"] += ns * 24
            n["h"] += ns * 12
            n["sg"] += ns * 12
            n["group"] += ns
        elif s["kind"] == "attn":
            n["unit"] += 6 + 2 + 4
            n["inq"] += 8
            n["group"] += 1
            n["tile"] += TT - 1
            n["item"] += HEADS * TT
        else:
            n["unit"] += 12 + 4
            n["inq"] += 12
            n["group"] += 1
            n["tile"] += TT - 1
            n["item"] += M_HEADS * TT
            n["mix"] += 1
    return subs


class Items(list):

    def __init__(self, block):
        self.d, self.masked = (HD, False) if block == 1 else (M_HD, True)
        n = HEADS if block == 1 else M_HEADS
        super().__init__((h, t, (t + 1) * P if self.masked else 2 * T) for h in range(n) for t in range(TT))
        self.scale = 1.0 if self.masked else self.d ** -0.5


class Stages:

    def __init__(self, sem, names):
        self.sem, self.names, self.at = sem, names.split(), 0

    def done(self, name, ins):
        self.skip(name)
        ins.then_inc(self.sem, 1)

    def skip(self, name):
        assert self.names[self.at] == name, (name, self.names[self.at])
        self.at = (self.at + 1) % len(self.names)

    def wait(self, eng, name, turn):
        eng.wait_ge(self.sem, turn * len(self.names) + self.names.index(name) + 1)


class Steps:

    def __init__(self, eng, sem, start=0):
        self.eng, self.sem, self.n, self.loop = eng, sem, start, None

    def value(self, n=None):
        n = self.n if n is None else n
        return n if self.loop is None else n + self.loop[0] * self.loop[1]

    def mark(self, ins):
        ins.then_inc(self.sem, 1)
        self.n += 1
        return self.n

    def wait(self, n):
        self.eng.wait_ge(self.sem, self.value(n))

    def link(self, ins):
        self.wait(self.mark(ins))

    def enter(self, i, each):
        self.loop = (i, each)
        self.first = self.n

    def leave(self, times):
        i, each = self.loop
        assert self.n - self.first == each, (self.n - self.first, each)
        self.n, self.loop = self.first + each * times, None


def program(nc, ins, out, subs):
    u_end = subs[-1]["n_unit"] + dict(ffn=33, gmlp=72, attn=12, mix=16)[subs[-1]["kind"]]
    with ExitStack() as ctx:
        def sb(name, shape, dt=F32):
            return ctx.enter_context(nc.sbuf_tensor(name, shape, dt))

        def sem(name):
            return ctx.enter_context(nc.semaphore(name))

        x = sb("x", [P, 2, TT, D])
        wraw = sb("wraw", [P, 2, 2048])
        wh = sb("wh", [P, 2, 2048], F32R)
        wl = sb("wl", [P, 2, 2048], F32R)
        mraw = sb("mraw", [P, 2, 2, D])
        acc = sb("acc", [P, 2, D])
        biasrow = sb("biasrow", [P, D])
        gate = sb("gate", [P, 2, D])
        lnp = sb("lnp", [P, 2, D])
        modc = sb("modc", [P, 2, 3, 2, KD])
        prea = sb("prea", [P, 2, KD])
        gaincol = sb("gaincol", [P, KD])
        lncol = sb("lncol", [P, 2, KD])
        cvec = sb("cvec", [P, 3, KD])
        svec = sb("svec", [P, 3, KD])
        sg = sb("sg", [P, 2, 512])
        ht = sb("ht", [P, 2, 512])
        ident = sb("ident", [P, P])
        ones = sb("ones", [P, P])
        st = sb("st", [P, TT, 12, 6])
        mv = sb("mv", [P, TT, 2])
        rstd = sb("rstd", [P, TT])
        wst = sb("wst", [P, SG_GROUPS, P])
        zeros = sb("zeros", [P, P], F32R)
        scrap = sb("scrap", [P, TT])
        mhalf = sb("mhalf", [P, TT * 16])
        nrm = sb("nrm", [P, TT, 16])
        negm = sb("negm", [P, 16])
        den = sb("den", [P, 2, 16])
        hgain = sb("hgain", [P, 2, HD])
        rope = sb("rope", [P, TT, 2, HD // 2])
        rope2 = sb("rope2", [P, 2, TT, M_HD // 2])
        pos = sb("pos", [P, TT], I32)
        cgh_, cgl_ = sb("cgh", [P, KD * 16], F32R), sb("cgl", [P, KD * 16], F32R)
        cgh, cgl = cgh_[:], cgl_[:]

        def alias(*shapes):
            with ExitStack() as a:
                return [a.enter_context(nc.sbuf_tensor(n, s, d)) for n, s, d in shapes]
        xh, xl = alias(("xh", [P, KD, 2 * T], F32R), ("xl", [P, KD, 2 * T], F32R))
        qt_t, kt_t, qeo, sc_t, kvs, sts, cg_t = alias(
            ("qt_t", [64, G_HEADS, T], F32), ("kt_t", [64, G_HEADS, T], F32), ("qeo", [64, 2, G_HEADS, T], F32),
            ("sc_t", [P, TT * G_HEADS, P], F32), ("kvs", [64, G_HEADS, 4, G_D], F32),
            ("sts", [64, G_HEADS, 3, G_D], F32), ("cg_t", [32, T], F32))
        _, ch_t, cw_t = alias(("before_ch_t", [P, 7168], F32), ("ch_t", [P, 2, T + 32], F32), ("cw_t", [P, 2, 32], F32))
        q2, k2, tm2, cacc, ctok = alias(
            ("q2", [64, M_HEADS, T], F32), ("k2", [64, M_HEADS, T], F32), ("tm2", [P, 2, 256], F32),
            ("cacc", [P, 2, T], F32), ("ctok", [P, TT, 256], F32))
        sb("place_of_inputs", [P, 2 * KD * 2 * T])
        hh, hl = alias(("hh", [P, 12 * 512], F32R), ("hl", [P, 12 * 512], F32R))
        _, zt0, _, zt1 = alias(("hh_", [P, 10 * 512], F32), ("zt0", [P, D], F32),
                               ("hl_", [P, 10 * 512], F32), ("zt1", [P, D], F32))
        zt = (zt0, zt1)
        zm = (mraw[:, 0, 0], mraw[:, 1, 0])
        first_w, = alias(("first_w", [P, 6, 2, D], F32))
        ptmp, z = alias(("ptmp", [P, 2, KD, T], F32), ("z", [P, TT, D], F32))
        _, v0, vg, _, v1, gb = alias(("gm_hh", [P, 1536], F32), ("v0", [P, GM_HALF], F32),
                                     ("vg", [P, TT, GM_GROUP], F32), ("gm_hl", [P, 1536], F32),
                                     ("v1", [P, GM_HALF], F32), ("gb", [P, 2, GM_GROUP], F32))
        v = (v0, v1)
        ql, kvc, _, qt1, kt1, tm1 = alias(("ql", [P, TT, QKV], F32), ("kvc", [P, TT, 2 * KV_HEADS * HD], F32),
                                        ("at_z", [P, TT, D], F32), ("qt1", [P, HEADS, T], F32),
                                        ("kt1", [P, KV_HEADS, 2 * T], F32), ("tm1", [P, 2, 1280], F32))
        proj, om, gg, e1, e2, e3, kt, ke, hx = alias(
            ("proj", [P, TT, 3072], F32), ("om", [P, TT, D], F32), ("gg", [P, TT, 256], F32),
            ("e1", [P, TT, 256], F32), ("e2", [P, TT, 256], F32), ("e3", [P, TT, 256], F32),
            ("kt", [P, TT, 256], F32), ("ke", [P, 2, TT, 256], F32), ("hx", [P, TT, 256], F32))
        bsrow = mraw[0:1, 0, 0]
        ps = ctx.enter_context(nc.psum_tensor("ps", [P, 8, 512], F32))
        place = x[:, 1].rearrange("p t d -> p (t d)")
        causal, tri, suf = (place[:, i * P:(i + 1) * P] for i in range(3))
        conv_raw, gate_raw = place[0:32, 512:768], place[0:32, 768:1024]
        conv_norm = place[:, 1024:1536].rearrange("p (a b) -> p a b", a=2)
        out_norm, cg_raw = place[:, 1536:1600], place[:, 1600:1728]
        pos_f = place[:, 1728:1730]
        decay = place[0:64, 1760:1776]
        freqs = place[:, 1776:1808]
        hst = place[:, 1808:1856].rearrange("p (a b) -> p a b", a=8)
        hmv = place[:, 1856:1872].rearrange("p (a b) -> p a b", a=8)
        hrs = place[:, 1872:1880]
        nrm_g = place[:, 1944:1952]
        tm_ang = place[:, 1880:1944].rearrange("p (t f) -> p t f", t=TT)
        ang = place[:, 384:512].rearrange("p (a t f) -> p a t f", a=2, t=TT)

        wraw_full = [sem("wraw_full0"), sem("wraw_full1")]
        whi_done, wlo_done = sem("whi_done"), sem("wlo_done")
        w_used = sem("w_used")
        mraw_full = [sem("mraw_full0"), sem("mraw_full1")]
        mod_used = sem("mod_used")
        first_full = [sem("first_full%d" % i) for i in range(6)]
        first_used, first_bias, first_rows = sem("first_used"), sem("first_bias"), sem("first_rows")
        bias_full, bias_used = sem("bias_full"), sem("bias_used")
        cols_ready, mcol_done = sem("cols_ready"), sem("mcol_done")
        gate_ps = sem("gate_ps")
        pair_free = sem("pair_free")
        sg_ready, h_ready = sem("sg_ready"), sem("h_ready")
        y_tile = sem("y_tile")
        y_evac = sem("y_evac")
        x_ready, z_ready = sem("x_ready"), sem("z_ready")
        tr_done = sem("tr_done")
        tr_act, tr_dve = sem("tr_act"), sem("tr_dve")
        x_mod = sem("x_mod")
        pre_hi, pre_ready = sem("pre_hi"), sem("pre_ready")
        ssq_ready, var_ready, rstd_ready = sem("ssq_ready"), sem("var_ready"), sem("rstd_ready")
        ln_full, ln_used = sem("ln_full"), sem("ln_used")
        col_full = sem("col_full")
        gain_full, gain_used = sem("gain_full"), sem("gain_used")
        in_full, ident_ready, svec_ready = sem("in_full"), sem("ident_ready"), sem("svec_ready")
        vstep, pstep, astep = sem("vstep"), sem("pstep"), sem("astep")
        out_full = sem("out_full")
        ws_full, wst_ps, wst_ready = sem("ws_full"), sem("wst_ps"), sem("wst_ready")
        bs_full, y_closed = sem("bs_full"), sem("y_closed")
        gb_full, gb_used, vg_ready = sem("gb_full"), sem("gb_used"), sem("vg_ready")
        s_ps, max_ready, p_ready = sem("s_ps"), sem("max_ready"), sem("p_ready")
        pt_ps, pt_ready = sem("pt_ps"), sem("pt_ready")
        o_ps, o_taken = sem("o_ps"), sem("o_taken")
        att_full = sem("att_full")
        AA = Stages(sem("attention_act"), "heads")
        AV = Stages(sem("attention_dve"), "shaped heads")
        AP_ = Stages(sem("attention_pe"), "heads")
        mix_full, ang_ready, rope2_ready = sem("mix_full"), sem("ang_ready"), sem("rope2_ready")
        MA = Stages(sem("mix_act"), "cgh sig ch_t softplus decays qt_t silu cacc q2 conv")
        MV = Stages(sem("mix_dve"), "cgl h cg_t absz g qk kt_t states shaped o_copy oc k2 stats o_conv")
        MP = Stages(sem("mix_pe"), "cg h_t z sums qk_t scores o taps heads conv")
        MG = Stages(sem("mix_pool"), "masks zeroed")
        tap_ready, tap_used = sem("tap_ready"), sem("tap_used")
        block = ctx.enter_context(nc.Block())

        def mod_of(s):
            w, b = ("w_mod", "b_mod") if s["block"] == 1 else ("ada_w_2", "ada_b_2")
            return ins[w][s["layer"]].rearrange("(p j) n -> p j n", j=KD), ins[b], 3 * D * s["part"]

        def conds(s):
            return (0, 1)[:len(s["streams"])]

        def ffn_w(s):
            l = s["layer"]
            if s["block"] == 1:
                return ins["ffn_w_in"][l, s["part"] // 2], ins["ffn_w_out"][l, s["part"] // 2]
            n = "ffn1" if s["part"] == 0 else "ffn2"
            return ins[n + "_w_in_2"][l], ins[n + "_w_out_2"][l]

        def mods_taken(per, j, i):
            return [(i, q) for q in ((0, 1), (2,), (3,), ())[j]] if per == 4 else [(j // 2, 2 * (j % 2) + q) for q in (0, 1)]

        def mods_loaded(per, j, i):
            if per == 4:
                return [(i, q) for q in ((0,), (1,), (), (2, 3))[j]]
            n = j - 2 if j else 0
            return [] if j in (1, 2) else mods_taken(per, n, i)

        def section_done(per, j, i):
            sec = (i if j == per - 1 else None) if per == 4 else (j // 2 if j % 2 else None)
            return None if isinstance(sec, int) and sec == 2 else sec

        def mod_loop(eng, n, per, body, mods, steps=None, each=0):
            if mods is None or per != 4:
                loop(eng, n, per, body, steps, each)
            else:
                loop(eng, n - per, per, body, steps, each)
                for j in range(per):
                    body(n - per + j, j, 2)

        def unscaled(s):
            return s is not None and s["block"] == 1 and s["i"] > 0

        def after(s):
            return subs[s["i"] + 1] if s["i"] + 1 < len(subs) else None

        def loop(eng, n, per, body, steps=None, each=0):
            turns = n // per
            if turns > 1:
                with eng.Fori(0, turns) as i:
                    if steps:
                        steps.enter(i, each)
                    for j in range(per):
                        body(i * per + j, j, i)
                if steps:
                    steps.leave(turns)
            else:
                for j in range(turns * per):
                    body(j, j, 0)
            for j in range(n - turns * per):
                body(turns * per + j, j, turns)

        @block.sync
        def _(sp):
            unit = [FIRST]

            def load_mod(s, sec, q, mu):
                w, b, off = mod_of(s)
                if q == 0:
                    sp.wait_ge(bias_used, sec + (3 * s["i"] + 1))
                    sp.dma_start(biasrow[0:1, :], b[s["layer"]:s["layer"] + 1, bass.ds(sec * D + off, D)])\
                        .then_inc(bias_full, 16)
                sp.wait_ge(mod_used, mu)
                sp.dma_start(mraw[:, q % 2], w[:, 2 * q:2 * q + 2, bass.ds(sec * D + off, D)])\
                    .then_inc(mraw_full[q % 2], 16)

            def load(u, count, halves, by_column=False):
                slot = u % 2
                sp.wait_ge(wlo_done, count)
                for half, a in enumerate(halves):
                    n_a, n_b = a.shape[1], a.shape[2]
                    if by_column:
                        dst = wraw[:, slot].rearrange("p (a t b) -> p a t b", t=2, b=n_b)[:, :, half]
                    else:
                        dst = wraw[:, slot, half * n_a * n_b:(half + 1) * n_a * n_b]\
                            .rearrange("p (a b) -> p a b", a=n_a)
                    sp.dma_start(dst, a).then_inc(wraw_full[slot], 16)

            def phase(n, per, src, mods=None, by_column=False):
                u0 = unit[0]

                def body(idx, j, i):
                    load(u0 + j, idx + u0, src(idx), by_column)
                    if mods is not None:
                        for sec, q in mods_loaded(per, j, i):
                            load_mod(mods, sec, q, sec * 4 + (12 * mods["i"] + q + 1))
                loop(sp, n, per, body)
                unit[0] += n

            for full in wraw_full:
                sp.sem_inc(full, 16 * FIRST)
            for full in mraw_full:
                sp.sem_inc(full, 64)
            sp.sem_inc(bias_full, 32)
            for k, name in enumerate(("c", "c_ctx", "c_2")):
                v = ins[name]
                v = v.rearrange("a n -> (a n)") if len(v.shape) == 2 else v
                sp.dma_start(cvec[:, k], v.rearrange("(p j) -> p j", j=KD)).then_inc(in_full, 16)
            sp.dma_start(x[:, 0], ins["x"][0].rearrange("(t p) d -> p t d", p=P)).then_inc(in_full, 16)
            sp.dma_start(x[:, 1], ins["ctx"][0].rearrange("(t p) d -> p t d", p=P)).then_inc(in_full, 16)
            sp.dma_start(ht[:].rearrange("p a b -> p (a b)").rearrange("p (g q) -> p g q", g=SG_GROUPS),
                         ins["gmlp_w_s"][0].rearrange("g p q -> p g q")).then_inc(ws_full, 16)
            w, b, off = mod_of(subs[0])
            sp.dma_start(gate[0:2].rearrange("p a b -> p (a b)"), b[subs[0]["layer"], off:off + 2 * D].partition_broadcast(2))\
                .then_inc(first_bias, 16)
            for n in range(8):
                if n % 2 == 0:
                    load_mod(subs[0], 2, n // 2, n // 2 + 9)
                if n >= 6:
                    sp.wait_ge(first_used, n - 5)
                at = off + n // 4 * D
                sp.dma_start(first_w[:, n % 6], w[:, 2 * (n % 4):2 * (n % 4) + 2, at:at + D]).then_inc(first_full[n % 6], 16)
            for s in subs:
                nxt = after(s)
                if s["kind"] == "ffn":
                    w_in, w_out = ffn_w(s)
                    w_in = w_in.rearrange("(k p) (t m c) -> p k t m c", p=P, t=2, c=P)
                    w_out = w_out.rearrange("(m p) n -> p m n", p=P)
                    m0 = 0
                    for g, n in enumerate(GROUPS):
                        phase(n, 2 if g else 4, lambda idx: [
                            w_in[:, :, t, bass.ds(idx + m0, 1), :].rearrange("p k m c -> p k (m c)")
                            for t in range(2)], None if g else nxt, by_column=True)
                        phase(n // 2, 2, lambda idx: [w_out[:, bass.ds(idx * 2 + (m0 + kk), 1), :] for kk in range(2)])
                        m0 += n
                elif s["kind"] == "gmlp":
                    w_in = ins["gmlp_w_in"][0].rearrange("(k p) n -> p k n", p=P)
                    w_out = ins["gmlp_w_out"][0].rearrange("(m p) n -> p m n", p=P)
                    lng, lnb = ins["gmlp_ln_g"][0], ins["gmlp_ln_b"][0]
                    for k, c in enumerate(s["streams"]):
                        phase(12, 4, lambda idx: [w_in[:, kk:kk + 4, bass.ds(idx * CW + GM_HALF, CW)]
                                                  for kk in (0, 4)], nxt if k == 0 else None)
                        if k == 0:
                            sp.wait_ge(mod_used, 12 * (s["i"] + 2) + 2)
                            sp.dma_start(bsrow, ins["gmlp_b_s"].rearrange("a g p -> a (g p)")).then_inc(bs_full, 16)
                        u0 = unit[0]

                        def group(idx, j, i):
                            sp.wait_ge(gb_used, idx + (GM_STEPS * k + 1))
                            for b, a in enumerate((lng, lnb)):
                                row = a[bass.ds(idx * GM_GROUP, GM_GROUP)].partition_broadcast(P)
                                sp.dma_start(gb[:, b], row).then_inc(gb_full, 16)
                            for q in range(3):
                                load(u0 + q, idx * 6 + (u0 + q),
                                     [w_in[:, kk:kk + 4, bass.ds(idx * GM_GROUP + q * CW, CW)] for kk in (0, 4)])
                            for q in range(3):
                                load(u0 + 3 + q, idx * 6 + (u0 + 3 + q),
                                     [w_out[:, bass.ds(idx * 6 + (2 * q + kk), 1), :] for kk in range(2)])
                        loop(sp, GM_STEPS, 1, group)
                        unit[0] += 6 * GM_STEPS
                    sp.wait_ge(w_used, unit[0])
                elif s["kind"] == "attn":
                    for g, name in enumerate(("attn_q_norm", "attn_k_norm")):
                        sp.dma_start(hgain[:, g], ins[name][0].partition_broadcast(P)).then_inc(att_full, 16)
                    for t in range(TT):
                        sp.dma_start(rope[:, t], ins["rope_1"].rearrange("a (t p) d -> p t a d", p=P)[:, t])\
                            .then_inc(att_full, 16)
                    w_in = ins["attn_w_qkv"][0].rearrange("(k p) n -> p k n", p=P)
                    w_out = ins["attn_w_o"][0].rearrange("(m p) n -> p m n", p=P)
                    phase(8, 8, lambda idx: [w_in[:, kk:kk + 4, bass.ds((idx if idx < 6 else idx - 2) * CW, CW)]
                                             for kk in (0, 4)], nxt)
                    phase(4, 2, lambda idx: [w_out[:, bass.ds(idx * 2 + kk, 1), :] for kk in range(2)])
                elif s["kind"] == "mix":
                    w_in = ins["mix_w_in_2"][s["layer"]].rearrange("(k p) n -> p k n", p=P)
                    w_out = ins["mix_w_out_2"][s["layer"]].rearrange("(m p) n -> p m n", p=P)
                    phase(12, 4, lambda idx: [w_in[:, kk:kk + 4, bass.ds(idx * CW, CW)] for kk in (0, 4)], nxt)
                    phase(4, 2, lambda idx: [w_out[:, bass.ds(idx * 2 + kk, 1), :] for kk in range(2)])
            sp.wait_ge(x_ready, subs[-1]["n_pre"] + len(subs[-1]["streams"]) + 1)
            sp.dma_start(out[0].rearrange("(t p) d -> p t d", p=P), x[:, 0]).then_inc(out_full, 16)
            sp.wait_ge(out_full, 16)

        @block.gpsimd
        def _(pool):
            steps = Steps(pool, pstep)
            steps.link(pool.memset(ident[:], 0.0))
            steps.link(pool.affine_select(out=ident[:], in_=ident[:], compare_op=ALU.not_equal, fill=1.0, base=0,
                                          pattern=[[-1, P]], channel_multiplier=1))
            pool.memset(ones[:], 1.0).then_inc(ident_ready, 1)
            steps.link(pool.memset(mhalf[:], -0.5))
            pool.memset(zeros[:].bitcast(F32), 0.0).then_inc(ident_ready, 1)
            n_power = [0]

            def power(what=rstd[:], n=TT):
                n_power[0] += 1
                pool.wait_ge(var_ready, n_power[0])
                pool.tensor_tensor(what, what, mhalf[:, 0:n], ALU.pow).then_inc(rstd_ready, 1)

            def split(where, par, width):
                steps.link(pool.tensor_copy(hh[:, where], ht[:, par, 0:width]))
                pool.tensor_tensor(hl[:, where], ht[:, par, 0:width], hh[:, where].bitcast(F32), ALU.subtract)\
                    .then_inc(h_ready, 1)

            def split_h(n, q0, h0, width, at):
                def body(idx, j, i):
                    pool.wait_ge(pair_free, idx + (q0 + 2))
                    split(bass.ds(idx * width + at, width), (q0 + j) % 2, width)
                loop(pool, n, 2, body, steps, 2)

            def load_ln(s):
                pool.wait_ge(ln_used, s["i"])
                for k, name in enumerate(("ln_g", "ln_b")):
                    pool.dma_start(lnp[:, k], ins[name][s["layer"], s["part"]].partition_broadcast(P)).then_inc(ln_full, 16)

            for s in subs:
                if s["block"] == 2:
                    pool.wait_ge(gain_used, s["i"] - B2)
                    g = ins[{0: "ffn1_norm_2", 1: "mix_norm_2", 2: "ffn2_norm_2"}[s["part"]]][s["layer"]]
                    with nc.allow_non_contiguous_dma("a column of 1024 gains"):
                        pool.dma_start(gaincol[:], g.rearrange("(k p) -> p k", p=P)).then_inc(gain_full, 16)
                    power()
                elif unscaled(after(s)):
                    pool.wait_ge(x_mod, s["i"] + 1)
                    with nc.allow_non_contiguous_dma("columns of 1024"):
                        for k, name in enumerate(("ln_g", "ln_b")):
                            pool.dma_start(lncol[:, k], ins[name][s["layer"], s["part"]].rearrange("(k p) -> p k", p=P))\
                                .then_inc(col_full, 16)
                if s["kind"] == "ffn":
                    m0 = 0
                    for g, n in enumerate(GROUPS):
                        pool.wait_ge(w_used, s["n_unit"] + 18 * g)
                        split_h(n, s["n_inq"] + m0, s["n_h"] + m0, T * len(s["streams"]), 0)
                        if g == 0 and s["block"] == 1:
                            load_ln(s)
                        m0 += n
                elif s["kind"] == "gmlp":
                    for k, c in enumerate(s["streams"]):
                        u0, q0 = s["n_unit"] + 36 * k + 12, s["n_inq"] + 24 * k + 12
                        power()

                        def group(idx, j, i):
                            pool.wait_ge(w_used, idx * 6 + u0)
                            for q in range(3):
                                pool.wait_ge(pair_free, idx * 3 + (q0 + q + 2))
                                pool.tensor_tensor(scrap[:], mhalf[:, 0:TT], mhalf[:, 0:TT], ALU.add)
                                split(slice(q * 512, (q + 1) * 512), q % 2, 512)
                        loop(pool, GM_STEPS, 1, group, steps, 3)
                    load_ln(s)
                elif s["kind"] == "attn":
                    power(nrm[:].rearrange("p a b -> p (a b)"), TT * 16)
                    power(negm[:, 0:TT * KV_HEADS], TT * KV_HEADS)
                    load_ln(s)
                elif s["kind"] == "mix":
                    turn, l = s["n_mix"], s["layer"]
                    pool.wait_ge(x_ready, s["n_pre"] + 1)
                    loads = [(cg_raw.rearrange("p (k c) -> p k c", k=KD),
                              ins["mix_w_in_2"][l].rearrange("(k p) n -> p k n", p=P)[:, :, IN_W - 16:IN_W]),
                             (conv_raw[0:CONV_K], ins["conv_w_2"][l]), (conv_raw[CONV_K:CONV_K + 1], ins["conv_b_2"][l:l + 1]),
                             (gate_raw[0:16], ins["gla_gate_w_2"][l]), (gate_raw[16:17], ins["gla_gate_b_2"][l:l + 1]),
                             (out_norm, ins["gla_out_norm_2"][l].partition_broadcast(P)),
                             (hgain[:, 0, 0:M_HD], ins["q_norm_2"][l].partition_broadcast(P)),
                             (hgain[:, 1, 0:M_HD], ins["k_norm_2"][l].partition_broadcast(P)),
                             (conv_norm[:, 0], ins["conv_norm_g_2"][l].partition_broadcast(P)),
                             (conv_norm[:, 1], ins["conv_norm_b_2"][l].partition_broadcast(P))]
                    if turn == 0:
                        loads += [(pos[:], ins["positions_2"][0].rearrange("(t p) -> p t", p=P)),
                                  (freqs, ins["rope_freqs_2"][0].partition_broadcast(P))]
                    with nc.allow_non_contiguous_dma("small tables"):
                        for to, a in loads:
                            pool.dma_start(to, a).then_inc(mix_full, 16)
                    if turn == 0:
                        pool.memset(causal, 0.0)
                        pool.memset(tri, 1.0)
                        steps.link(pool.memset(suf, 1.0))
                        pool.affine_select(out=causal, in_=causal, compare_op=ALU.is_ge, fill=NEG, base=0,
                                           pattern=[[-1, P]], channel_multiplier=1)
                        pool.affine_select(out=tri, in_=tri, compare_op=ALU.is_ge, fill=0.0, base=0,
                                           pattern=[[1, P]], channel_multiplier=-1)
                        steps.link(pool.affine_select(out=suf, in_=suf, compare_op=ALU.is_ge, fill=0.0, base=-1,
                                                      pattern=[[-1, P]], channel_multiplier=1))
                        pool.memset(tri[0:64, 64:P], 0.0)
                        MG.done("masks", pool.memset(suf[64:P, 0:64], 0.0))
                    else:
                        MG.done("masks", pool.memset(scrap[:], 0.0))
                    MP.wait(pool, "cg", turn)
                    pool.memset(qeo[:], 0.0)
                    MG.done("zeroed", pool.memset(ch_t[:, :, 0:CONV_K - 1], 0.0))
                    power(nrm[:].rearrange("p a b -> p (a b)"), TT * 16)
                    power(nrm_g, TT * G_HEADS)
                    power(hrs, 8)
                if s["block"] == 1:
                    for c in s["post"]:
                        power()

        @block.scalar
        def _(act):
            steps = Steps(act, astep)

            def split_next(u, i=0, each=0):
                slot = (u + 1) % 2
                act.wait_ge(wraw_full[slot], i * (16 * each) + 32 * ((u + 1) // 2 + 1))
                act.wait_ge(w_used, i * each + u)
                act.activation(wh[:, slot], wraw[:, slot], ACT.Copy).then_inc(whi_done, 1)

            def phase(n, u0, per, evac=None):
                def body(idx, j, i, split=True):
                    if split:
                        split_next(u0 + idx) if isinstance(idx, int) else split_next(u0 + j, i, per)
                    if evac:
                        evac(idx, j, i)
                if u0 + n == u_end:
                    loop(act, n - 1, per, body)
                    body(n - 1, (n - 1) % per, 0, False)
                else:
                    loop(act, n, per, body)

            act.wait_ge(in_full, 5 * 16)
            act.activation(svec[:], cvec[:], ACT.Silu).then_inc(svec_ready, 1)
            act.sem_inc(whi_done, FIRST)
            act.wait_ge(wraw_full[0], 16 * FIRST + 32)
            act.activation(wh[:, 0], wraw[:, 0], ACT.Copy).then_inc(whi_done, 1)

            def prepare_half(s, k, c, source=None):
                r = s["n_tr"] + k
                act.wait_ge(tr_done, r + 1)
                act.wait_ge(x_mod, s["i"] + 1)
                for kc in range(4):
                    last = act.activation(ptmp[:, c, kc], ps[:, kc // 2, (kc % 2) * T:(kc % 2 + 1) * T], ACT.Identity,
                                          bias=modc[:, s["i"] % 2, 0, c, kc:kc + 1], scale=prea[:, c, kc:kc + 1])
                last.then_inc(tr_act, 1)
                split_input(r, c)

            def split_input(r, c):
                for half, ready in enumerate((tr_act, tr_dve)):
                    act.wait_ge(ready, r + 1)
                    act.activation(xh[:, 4 * half:4 * half + 4, c * T:(c + 1) * T], ptmp[:, c, 4 * half:4 * half + 4],
                                   ACT.Copy).then_inc(pre_hi, 1)

            def copies(u0, q0, to):
                def evac(idx, j, i):
                    pair = (q0 + j) % 2
                    act.wait_ge(w_used, idx + (u0 + 1))
                    act.activation(to[:, :, bass.ds(idx * CW, CW)], ps[:, 2 * pair:2 * pair + 2, 0:CW], ACT.Copy)\
                        .then_inc(pair_free, 1)
                return evac

            def exponentials(n0, items):
                for n, (h, t, keys) in enumerate(items):
                    act.wait_ge(max_ready, n0 + n + 1)
                    if n >= 2:
                        act.wait_ge(pt_ps, n0 + n - 1)
                    act.activation(sg[:, n % 2, 0:keys], ps[:, n % 2, 0:keys], ACT.Exp, bias=negm[:, n:n + 1],
                                   scale=items.scale, accum_out=den[:, 0, n:n + 1]).then_inc(p_ready, 1)

            def copy_output(r):
                act.wait_ge(tr_done, r + 1)
                act.activation(ptmp[:, 0, 0:4].rearrange("p a b -> p (a b)"),
                               ps[:, 0:2].rearrange("p a b -> p (a b)"), ACT.Copy).then_inc(tr_act, 1)
                split_input(r, 0)

            for s in subs:
                if s["block"] == 2:
                    act.wait_ge(x_ready, s["n_pre"] + 1)
                    for t in range(TT):
                        act.activation(z[:, t], x[:, 0, t], ACT.Square, accum_out=rstd[:, t:t + 1])\
                            .then_inc(ssq_ready, 1)
                for k, c in enumerate(s["streams"]):
                    prepare_half(s, k, c)
                if s["kind"] == "ffn":
                    W = T * len(s["streams"])
                    m0, u0 = 0, s["n_unit"]
                    for g, n in enumerate(GROUPS):
                        q0 = s["n_inq"] + m0

                        def evac(idx, j, i):
                            pair = (q0 + j) % 2
                            act.wait_ge(w_used, idx + (u0 + 1))
                            act.wait_ge(pair_free, idx + q0)
                            act.activation(sg[:, pair, 0:W], ps[:, 2 * pair, 0:W], ACT.Silu).then_inc(sg_ready, 1)
                        phase(n, u0, 2 if g else 4, evac)
                        phase(n // 2, u0 + n, 2)
                        m0 += n
                        u0 += n + n // 2
                elif s["kind"] == "gmlp":
                    for k, c in enumerate(s["streams"]):
                        u0, q0 = s["n_unit"] + 36 * k, s["n_inq"] + 24 * k

                        def gelu(idx, j, i):
                            pair = (q0 + j) % 2
                            act.wait_ge(w_used, idx + (u0 + 1))
                            for t in range(TT):
                                op = act.activation(v[t][:, bass.ds(idx * CW, CW)], ps[:, 2 * pair + t, 0:CW], ACT.Gelu)
                            op.then_inc(pair_free, 1)
                        if k:
                            act.wait_ge(y_evac, s["n_group"] + k)
                        phase(12, u0, 4, gelu)
                        u1, q1, g1 = u0 + 12, q0 + 12, s["n_sg"] + 12 * k

                        def group(idx, j, i):
                            for q in range(3):
                                split_next(u1 + q, idx, 6)
                                act.wait_ge(w_used, idx * 6 + (u1 + q + 1))
                                act.wait_ge(pair_free, idx * 3 + (q1 + q + (1 if q == 0 else 0)))
                                act.activation(sg[:, q % 2].rearrange("p (a b) -> p a b", a=2),
                                               ps[:, 2 * (q % 2):2 * (q % 2) + 2, 0:T], ACT.Gelu).then_inc(sg_ready, 1)
                            for q in range(3):
                                split_next(u1 + 3 + q, idx, 6)
                        loop(act, GM_STEPS, 1, group)
                elif s["kind"] == "attn":
                    u0, q0 = s["n_unit"], s["n_inq"]
                    phase(6, u0, 6, copies(u0, q0, ql))
                    phase(2, u0 + 6, 2, copies(u0 + 6, q0 + 6, kvc))
                    AP_.wait(act, "heads", 0)
                    act.activation(qt1[:, 0:4].rearrange("p a b -> p (a b)"), ps[:, 0:2].rearrange("p a b -> p (a b)"),
                                   ACT.Copy)
                    AA.done("heads", act.activation(kt1[:, 0], ps[:, 4], ACT.Copy))
                    exponentials(s["n_item"], Items(1))
                    copy_output(s["n_tr"] + 2)
                    phase(4, u0 + 8, 2)
                elif s["kind"] == "mix":
                    u0, q0, turn = s["n_unit"], s["n_inq"], s["n_mix"]

                    def stage(name, ins_):
                        MA.done(name, ins_)
                        MA.wait(act, name, turn)
                    phase(12, u0, 4, copies(u0, q0, proj))
                    act.wait_ge(mix_full, 160 * (turn + 1) + 32)
                    if turn == 0:
                        act.wait_ge(ang_ready, 1)
                        act.activation(rope2[:].rearrange("p a t f -> p (a t f)"), ang.rearrange("p a t f -> p (a t f)"),
                                       ACT.Sin).then_inc(rope2_ready, 1)
                    stage("cgh", act.activation(cgh, cg_raw, ACT.Copy))

                    def taps(start, end):
                        for n in range(start, end):
                            if n >= 8:
                                act.wait_ge(tap_used, 2 * CONV_K * turn + n - 7)
                            cc, tap = divmod(n, CONV_K)
                            act.activation(sg[:, n % 8 // 4, n % 4 * P:(n % 4 + 1) * P], ident[:], ACT.Copy,
                                           scale=cw_t[:, cc, tap:tap + 1]).then_inc(tap_ready, 1)
                    stage("sig", act.activation(hx[:], proj[:, :, 1792:2048], ACT.Sigmoid))
                    MP.wait(act, "h_t", turn)
                    act.activation(ch_t[:, :, CONV_K - 1:CONV_K - 1 + T], ps[:, 2].rearrange("p (a b) -> p a b", a=2), ACT.Copy)
                    stage("ch_t", act.activation(cw_t[:].rearrange("p a b -> p (a b)"), ps[:, 1, 0:64], ACT.Copy))
                    taps(0, 8)
                    MV.wait(act, "absz", turn)
                    steps.link(act.activation(e1[:], e1[:], ACT.Exp))
                    stage("softplus", act.activation(e1[:], e1[:], ACT.Ln, bias=ones[:, 0:1]))
                    taps(8, 16)
                    MP.wait(act, "sums", turn)
                    sums = [ps[:, b].rearrange("p (t c) -> p t c", t=TT) for b in (5, 6)]
                    act.activation(e1[:], sums[0], ACT.Exp)
                    act.activation(e2[:], sums[0], ACT.Exp, scale=-1.0)
                    act.activation(e3[:], sums[1], ACT.Exp)
                    stage("decays", act.activation(decay, ps[0:64, 7, 0:16], ACT.Exp))
                    taps(16, 24)
                    MP.wait(act, "qk_t", turn)
                    stage("qt_t", act.activation(qt_t[:].rearrange("p a b -> p (a b)"),
                                                 ps[0:64, 0:2].rearrange("p a b -> p (a b)"), ACT.Copy))
                    taps(24, 40)
                    stage("silu", act.activation(gg[:], proj[:, :, 2816:3072], ACT.Silu))
                    taps(40, 2 * CONV_K)
                    MP.wait(act, "taps", turn)
                    for cc in range(2):
                        last = act.activation(cacc[:, cc], ps[:, 3, cc * T:(cc + 1) * T], ACT.Identity,
                                              bias=cw_t[:, cc, CONV_K:CONV_K + 1])
                    stage("cacc", last)
                    MP.wait(act, "heads", turn)
                    stage("q2", act.activation(q2[:].rearrange("p a b -> p (a b)"),
                                               ps[0:64, 0:4].rearrange("p a b -> p (a b)"), ACT.Copy))
                    MV.wait(act, "o_conv", turn)
                    stage("conv", act.activation(om[:, :, 512:768], ctok[:], ACT.Silu))
                    exponentials(s["n_item"], Items(2))
                    copy_output(s["n_tr"] + 1)
                    phase(4, u0 + 12, 2)

        @block.vector
        def _(dve):
            steps = Steps(dve, vstep)
            dve.memset(st[:], 0.0).then_inc(gb_used, 1)
            dve.sem_inc(wlo_done, FIRST + 1)
            dve.sem_inc(pair_free, FIRST + 1)
            dve.sem_inc(h_ready, FIRST + 1)
            dve.sem_inc(w_used, FIRST)
            dve.sem_inc(mod_used, 2 + 8)
            steps.link(dve.memset(biasrow[:], 0.0))
            dve.sem_inc(bias_used, 1 + 2)

            def mod_unit(s, sec, q):
                cs = conds(s)
                n = 12 * s["i"]
                dve.wait_ge(mraw_full[q % 2], sec * 32 + 16 * (n // 2 + q // 2 + 1))
                if q == 0:
                    dve.wait_ge(bias_full, sec * 16 + 16 * (3 * s["i"] + 1))
                else:
                    dve.wait_ge(mod_used, sec * 4 + (n + q + 2))
                for jj in range(2):
                    for c in cs:
                        v = 2 if s["block"] == 2 else c
                        op = dve.scalar_tensor_tensor(out=acc[:, c], in0=mraw[:, q % 2, jj],
                                                      scalar=svec[:, v, 2 * q + jj:2 * q + jj + 1],
                                                      in1=biasrow[:] if q == jj == 0 else acc[:, c],
                                                      op0=ALU.mult, op1=ALU.add)
                    if jj == 1:
                        op.then_inc(mod_used, 1)
                    elif q == 0:
                        op.then_inc(bias_used, 1)
                        dve.wait_ge(bias_used, sec + (3 * s["i"] + 2))
                    else:
                        steps.link(op)

            def mod_end(s, sec):
                dve.wait_ge(cols_ready, sec + (2 * s["i"] + 1))
                nc_ = len(conds(s))
                dst = modc[:, s["i"] % 2, bass.ds(sec, 1), 0:nc_, :].rearrange("p a c k -> p (a c k)")
                dve.tensor_copy(dst, ps[:, 4, 0:nc_ * KD]).then_inc(mcol_done, 1)

            def split_next(u, i=0, each=0):
                slot = (u + 1) % 2
                dve.wait_ge(whi_done, i * each + (u + 2))
                dve.tensor_tensor(wl[:, slot], wraw[:, slot], wh[:, slot].bitcast(F32), ALU.subtract)\
                    .then_inc(wlo_done, 1)

            def phase(n, u0, per, evac=None, mods=None, marks=0):
                def body(idx, j, i, split=True):
                    if split:
                        split_next(u0 + idx) if isinstance(idx, int) else split_next(u0 + j, i, per)
                    if mods is not None:
                        for sec, q in mods_taken(per, j, i):
                            mod_unit(mods, sec, q)
                    if evac:
                        evac(idx, j, i)
                    if mods is not None and section_done(per, j, i) is not None:
                        mod_end(mods, section_done(per, j, i))
                each = marks + (3 if mods is not None else 0)
                if u0 + n == u_end:
                    loop(dve, n - 1, per, body, steps, each)
                    body(n - 1, (n - 1) % per, 0, False)
                else:
                    mod_loop(dve, n, per, body, mods, steps, each)

            def factors(s):
                b, nc_ = s["i"] % 2, len(conds(s))
                dve.wait_ge(mcol_done, 2 * s["i"] + 2)
                if unscaled(s):
                    dve.wait_ge(col_full, 32 * s["i"])
                    one, shift = modc[:, b, 1, 0:nc_], modc[:, b, 0, 0:nc_]
                    g, bias = (lncol[:, k].unsqueeze(1).broadcast_to([P, nc_, KD]) for k in range(2))
                    steps.link(dve.tensor_scalar(one, one, 1.0, None, ALU.add))
                    dve.tensor_tensor(prea[:, 0:nc_], one, g, ALU.mult)
                    steps.link(dve.tensor_tensor(one, one, bias, ALU.mult))
                    op = dve.tensor_tensor(shift, shift, one, ALU.add)
                elif s["block"] == 1:
                    op = dve.tensor_scalar(prea[:, 0:nc_], modc[:, b, 1, 0:nc_], 1.0, None, ALU.add)
                else:
                    dve.wait_ge(gain_full, 16 * (s["i"] - B2 + 1))
                    op = dve.scalar_tensor_tensor(out=prea[:, 0], in0=modc[:, b, 1, 0], scalar=1.0, in1=gaincol[:],
                                                  op0=ALU.add, op1=ALU.mult)
                op.then_inc(x_mod, 1)
                dve.wait_ge(x_mod, s["i"] + 1)
                if s["block"] == 2:
                    dve.sem_inc(gain_used, 1)

            def split_input(r, c):
                for half in range(2):
                    dve.wait_ge(pre_hi, 2 * r + 1 + half)
                    at = slice(4 * half, 4 * half + 4)
                    dve.tensor_tensor(xl[:, at, c * T:(c + 1) * T], ptmp[:, c, at],
                                      xh[:, at, c * T:(c + 1) * T].bitcast(F32), ALU.subtract).then_inc(pre_ready, 1)

            def prepare_half(s, k, c):
                r = s["n_tr"] + k
                dve.wait_ge(tr_done, r + 1)
                for kc in range(4, 8):
                    last = dve.tensor_scalar(ptmp[:, c, kc], ps[:, kc // 2, (kc % 2) * T:(kc % 2 + 1) * T],
                                             prea[:, c, kc:kc + 1], modc[:, s["i"] % 2, 0, c, kc:kc + 1],
                                             ALU.mult, ALU.add)
                last.then_inc(tr_dve, 1)
                dve.wait_ge(tr_dve, r + 1)
                split_input(r, c)

            def gates(s):
                dve.wait_ge(gate_ps, s["i"] + 1)
                for c in range(len(s["post"])):
                    op = dve.tensor_scalar(gate[:, c], ps[:, 4 + 2 * c:6 + 2 * c].rearrange("p a b -> p (a b)"),
                                           0.5 if s["kind"] == "ffn" else 1.0, None, ALU.mult)
                steps.link(op)

            def take_y(s, streams, bank0, u, first, tiles=None, by=zt):
                n = TT * len(streams)
                if tiles is None:
                    dve.wait_ge(w_used, u)
                for i in range(n):
                    k, t = divmod(i, TT)
                    c = streams[k]
                    if tiles is not None and i < n - 1:
                        dve.wait_ge(y_tile, tiles + i + 1)
                    elif tiles is not None:
                        dve.wait_ge(w_used, u)
                    b = bank0 + 2 * i
                    if i >= TT:
                        steps.wait(last)
                    steps.link(dve.tensor_tensor(by[t][:], ps[:, b:b + 2].rearrange("p a b -> p (a b)"), gate[:, c], ALU.mult))
                    if i == n - 1:
                        dve.sem_inc(y_evac, 1)
                    last = steps.mark(dve.scalar_tensor_tensor(
                        out=x[:, c, t], in0=x[:, c, t], scalar=ALPHA if first and s["block"] == 1 else 1.0,
                        in1=by[t][:], op0=ALU.mult, op1=ALU.add))
                steps.wait(last)

            n_power = [0]

            def scale_x(s, streams):
                if not unscaled(s):
                    return
                dve.wait_ge(ln_full, 32 * s["i"])
                gain_and_bias(streams)

            def gain_and_bias(streams):
                for c in streams:
                    for k, op in enumerate((ALU.mult, ALU.add)):
                        for t in range(TT):
                            if k:
                                steps.wait(m - 1)
                            m = steps.mark(dve.tensor_tensor(x[:, c, t], x[:, c, t], lnp[:, k], op))
                    steps.wait(m)

            def layer_norm(s):
                for c in s["post"]:
                    for t in range(TT):
                        for half in range(2):
                            m = steps.mark(dve.bn_stats(st[:, t, half], x[:, c, t, half * 512:(half + 1) * 512]))
                    steps.wait(m)
                    for t in range(TT):
                        m = steps.mark(dve.bn_aggr(mv[:, t], st[:, t, 0:2]))
                    steps.wait(m)
                    dve.tensor_scalar(rstd[:], mv[:, :, 1], LN_EPS, None, ALU.add).then_inc(var_ready, 1)
                    n_power[0] += 1
                    dve.wait_ge(rstd_ready, n_power[0])
                    for t in range(TT):
                        m = steps.mark(dve.tensor_scalar(x[:, c, t], x[:, c, t], mv[:, t, 0:1], rstd[:, t:t + 1],
                                                         ALU.subtract, ALU.mult))
                    steps.wait(m)
                    if not unscaled(after(s)):
                        dve.wait_ge(ln_full, 32 * (s["i"] + 1))
                        gain_and_bias([c])
                    dve.sem_inc(x_ready, 1)

            def root_mean_square(s):
                dve.wait_ge(ssq_ready, TT * (s["i"] - B2 + 1))
                dve.tensor_scalar(rstd[:], rstd[:], 1.0 / D, RMS_EPS, ALU.mult, ALU.add).then_inc(var_ready, 1)
                n_power[0] += 1
                dve.wait_ge(rstd_ready, n_power[0])
                for t in range(TT):
                    m = steps.mark(dve.tensor_scalar(z[:, t], x[:, 0, t], rstd[:, t:t + 1], None, ALU.mult))
                steps.wait(m)
                dve.sem_inc(z_ready, 1)

            def head_squares(src, nh, d, to, buf):
                steps.link(dve.tensor_tensor(buf[:, 0:nh * d], src, src, ALU.mult))
                return steps.mark(dve.reduce_sum(to, buf[:, 0:nh * d].rearrange("p (h d) -> p h d", h=nh), axis=AX.X))

            def ask_factors(sums, d):
                steps.link(dve.tensor_scalar(sums, sums, 1.0 / d, RMS_EPS, ALU.mult, ALU.add))
                dve.sem_inc(var_ready, 1)
                n_power[0] += 1

            def norm_heads(a, nh, d, factor, gain):
                a = a.rearrange("p (h d) -> p h d", h=nh)
                steps.link(dve.tensor_tensor(a, a, factor.unsqueeze(2).broadcast_to([P, nh, d]), ALU.mult))
                steps.link(dve.tensor_tensor(a, a, gain.unsqueeze(1).broadcast_to([P, nh, d]), ALU.mult))

            def rotate_heads(a, nh, d, cos, sin, buf):
                half = d // 2
                a = a.rearrange("p (h r d) -> p h r d", h=nh, r=2)
                lo, hi = a[:, :, 0], a[:, :, 1]
                c, s_ = (w.unsqueeze(1).broadcast_to([P, nh, half]) for w in (cos, sin))
                b = buf[:, 0:nh * d].rearrange("p (r h d) -> p r h d", r=2, h=nh)
                dve.tensor_tensor(b[:, 0], lo, s_, ALU.mult)
                steps.link(dve.tensor_tensor(b[:, 1], hi, s_, ALU.mult))
                dve.tensor_tensor(lo, lo, c, ALU.mult)
                steps.link(dve.tensor_tensor(hi, hi, c, ALU.mult))
                dve.tensor_tensor(lo, lo, b[:, 1], ALU.subtract)
                steps.link(dve.tensor_tensor(hi, hi, b[:, 0], ALU.add))

            def softmax_items(n0, items, to):
                def maximum(n):
                    h, t, keys = items[n]
                    dve.wait_ge(s_ps, n0 + n + 1)
                    top = dve.tensor_reduce(negm[:, n:n + 1], ps[:, n % 2, 0:keys], axis=AX.X, op=ALU.max, negate=True)
                    if items.scale != 1.0:
                        steps.link(top)
                        top = dve.tensor_scalar(negm[:, n:n + 1], negm[:, n:n + 1], items.scale, None, ALU.mult)
                    top.then_inc(max_ready, 1)

                for n in range(2):
                    maximum(n)
                for n, (h, t, keys) in enumerate(items):
                    dve.wait_ge(pt_ps, n0 + n + 1)
                    dve.tensor_copy(ht[:, n % 2, 0:keys], ps[:, 2 + n % 2, 0:keys]).then_inc(pt_ready, 1)
                    if n + 2 < len(items):
                        maximum(n + 2)
                    steps.link(dve.reciprocal(den[:, 1, n:n + 1], den[:, 0, n:n + 1]))
                    dve.wait_ge(o_ps, n0 + n + 1)
                    dve.tensor_scalar(to[:, t, h * items.d:(h + 1) * items.d], ps[:, 4 + n % 2, 0:items.d],
                                      den[:, 1, n:n + 1], None, ALU.mult).then_inc(o_taken, 1)

            def copy_output(r):
                dve.wait_ge(tr_done, r + 1)
                dve.tensor_copy(ptmp[:, 0, 4:8].rearrange("p a b -> p (a b)"),
                                ps[:, 2:4].rearrange("p a b -> p (a b)")).then_inc(tr_dve, 1)
                dve.wait_ge(tr_dve, r + 1)
                split_input(r, 0)

            def rope_tables():
                posf, k, r = pos_f, ang[:, 0], ang[:, 1]
                steps.link(dve.tensor_copy(posf, pos[:]))
                a = tm_ang
                for t in range(TT):
                    m = steps.mark(dve.tensor_scalar(a[:, t], freqs, posf[:, t:t + 1], None, ALU.mult))
                steps.wait(m)
                steps.link(dve.tensor_scalar(k, a, 1.0 / (2 * np.pi), ROUND, ALU.mult, ALU.add))
                steps.link(dve.tensor_scalar(k, k, ROUND, None, ALU.subtract))
                for i, part in enumerate(TURN):
                    steps.link(dve.scalar_tensor_tensor(out=r, in0=k, scalar=-part, in1=r if i else a,
                                                        op0=ALU.mult, op1=ALU.add))
                steps.link(dve.tensor_scalar(k, r, np.pi / 2, None, ALU.add))
                steps.link(dve.tensor_scalar(a, k, np.pi, -2 * np.pi, ALU.is_gt, ALU.mult))
                steps.link(dve.tensor_tensor(k, k, a, ALU.add))
                steps.link(dve.tensor_scalar(ang, ang, PI_BELOW, -PI_BELOW, ALU.min, ALU.max))
                dve.sem_inc(ang_ready, 1)
                dve.wait_ge(rope2_ready, 1)

            dve.wait_ge(in_full, 5 * 16)
            dve.wait_ge(svec_ready, 1)

            for q in range(4):
                mod_unit(subs[0], 2, q)
            for half in range(2):
                dve.wait_ge(wst_ps, half + 1)
                dve.tensor_copy(wst[:, 4 * half:4 * half + 4].rearrange("p a b -> p (a b)"), ps[:, half])\
                    .then_inc(wst_ready, 1)
            nc_ = len(conds(subs[0]))
            for sec in range(2):
                dve.wait_ge(first_used, 4 * (sec + 1))
                dve.wait_ge(first_bias, 16)
                dve.tensor_tensor(gate[0:nc_, sec], ps[0:nc_, 4 + 2 * sec:6 + 2 * sec].rearrange("p a b -> p (a b)"),
                                  gate[0:nc_, sec], ALU.add).then_inc(first_rows, 1)
            for sec in range(2):
                dve.wait_ge(cols_ready, sec + 1)
                dve.tensor_copy(modc[:, 0, sec, 0:nc_], ps[:, 2 + sec, 0:nc_ * KD].rearrange("p (k c) -> p c k", c=nc_))\
                    .then_inc(mcol_done, 1)
            dve.sem_inc(x_ready, len(subs[0]["streams"]))
            dve.wait_ge(whi_done, FIRST + 1)
            dve.tensor_tensor(wl[:, 0], wraw[:, 0], wh[:, 0].bitcast(F32), ALU.subtract).then_inc(wlo_done, 1)
            for s in subs:
                nxt = after(s)
                if not unscaled(s):
                    factors(s)
                if s["block"] == 2:
                    root_mean_square(s)
                for k, c in enumerate(s["streams"]):
                    prepare_half(s, k, c)
                gates(s)
                if s["kind"] == "ffn":
                    W = T * len(s["streams"])
                    m0, u0 = 0, s["n_unit"]
                    for g, n in enumerate(GROUPS):
                        q0, h0 = s["n_inq"] + m0, s["n_h"] + m0
                        g0 = s["n_sg"] + m0

                        def evac(idx, j, i):
                            pair = (q0 + j) % 2
                            dve.wait_ge(sg_ready, idx + (g0 + 1))
                            dve.wait_ge(h_ready, idx + h0)
                            dve.tensor_tensor(ht[:, pair, 0:W], ps[:, 2 * pair + 1, 0:W], sg[:, pair, 0:W], ALU.mult)\
                                .then_inc(pair_free, 1)
                        phase(n, u0, 2 if g else 4, evac, None if g else nxt)
                        if g == 0:
                            scale_x(s, s["post"])
                            if unscaled(s):
                                dve.sem_inc(ln_used, 1)
                        elif unscaled(nxt):
                            factors(nxt)
                        phase(n // 2, u0 + n, 2)
                        u0 += n + n // 2
                        take_y(s, s["post"], 0 if W == 2 * T else 4, u0, g == 0, s["n_tile"] + g * (W // P - 1),
                               zt if g else zm)
                        m0 += n
                elif s["kind"] == "gmlp":
                    for k, c in enumerate(s["streams"]):
                        u0, q0 = s["n_unit"] + 36 * k, s["n_inq"] + 24 * k

                        def stats(idx, j, i):
                            dve.wait_ge(pair_free, idx + (q0 + 2))
                            for t in range(TT):
                                op = dve.bn_stats(st[:, t, bass.ds(idx, 1), :].rearrange("p a b -> p (a b)"),
                                                  v[t][:, bass.ds(idx * CW, CW)])
                            steps.mark(op)
                        phase(12, u0, 4, stats, nxt if k == 0 else None, 4)
                        steps.wait(steps.n)
                        for t in range(TT):
                            m = steps.mark(dve.bn_aggr(mv[:, t], st[:, t]))
                        steps.wait(m)
                        dve.tensor_scalar(rstd[:], mv[:, :, 1], LN_EPS, None, ALU.add).then_inc(var_ready, 1)
                        n_power[0] += 1
                        dve.wait_ge(rstd_ready, n_power[0])
                        u1, q1, g1, h1 = u0 + 12, q0 + 12, s["n_sg"] + 12 * k, s["n_h"] + 12 * k

                        def shape_group(idx):
                            dve.wait_ge(w_used, idx * 6 + (u1 - 3))
                            dve.wait_ge(gb_full, idx * 32 + 32 * (GM_STEPS * k + 1))
                            for t in range(TT):
                                m = steps.mark(dve.tensor_scalar(vg[:, t], v[t][:, bass.ds(idx * GM_GROUP, GM_GROUP)],
                                                                 mv[:, t, 0:1], rstd[:, t:t + 1],
                                                                 ALU.subtract, ALU.mult))
                            for b, op in enumerate((ALU.mult, ALU.add)):
                                for t in range(TT):
                                    steps.wait(m - 1)
                                    m = steps.mark(dve.tensor_tensor(vg[:, t], vg[:, t], gb[:, b], op))
                            steps.wait(m)
                            dve.sem_inc(gb_used, 1)
                            dve.sem_inc(vg_ready, 1)

                        def group(idx, last=False):
                            for q in range(3):
                                split_next(u1 + q, idx, 6)
                                dve.wait_ge(sg_ready, idx * 3 + (g1 + q + 1))
                                dve.wait_ge(h_ready, idx * 3 + (h1 + q + (1 if q == 0 else 0)))
                                dve.tensor_tensor(ht[:, q % 2].rearrange("p (a b) -> p a b", a=2),
                                                  ps[:, 2 * (q % 2):2 * (q % 2) + 2, T:2 * T],
                                                  sg[:, q % 2].rearrange("p (a b) -> p a b", a=2), ALU.mult)\
                                    .then_inc(pair_free, 1)
                            for q in range(3):
                                split_next(u1 + 3 + q, idx, 6)
                                if q == 0 and not last:
                                    shape_group(idx + 1)
                        shape_group(0)
                        loop(dve, GM_STEPS - 1, 1, lambda idx, j, i: group(idx), steps, 6)
                        group(GM_STEPS - 1, True)
                        scale_x(s, (c,))
                        if k == 0 and unscaled(nxt):
                            factors(nxt)
                        dve.wait_ge(y_closed, k + 1)
                        take_y(s, (c,), 4, u0 + 36, True)
                    if unscaled(s):
                        dve.sem_inc(ln_used, 1)
                elif s["kind"] == "attn":
                    u0, q0 = s["n_unit"], s["n_inq"]
                    steps.link(dve.memset(nrm[:], 1.0))
                    phase(6, u0, 6, None, nxt)

                    def latent_heads(idx, j, i):
                        if j == 0:
                            dve.wait_ge(pair_free, q0 + 7)
                            dve.wait_ge(att_full, 64)
                            for t in range(TT):
                                m = head_squares(ql[:, t, 0:1280], HEADS + KV_HEADS, HD, nrm[:, t, 0:10], tm1[:, t])
                            steps.wait(m)
                            ask_factors(nrm[:], HD)
                    phase(2, u0 + 6, 2, latent_heads)
                    dve.wait_ge(rstd_ready, n_power[0])

                    def latent_heads_shaped(t):
                        norm_heads(ql[:, t, 0:1024], HEADS, HD, nrm[:, t, 0:8], hgain[:, 0])
                        norm_heads(ql[:, t, 1024:1280], KV_HEADS, HD, nrm[:, t, 8:10], hgain[:, 1])
                        rotate_heads(ql[:, t, 0:1280], HEADS + KV_HEADS, HD, rope[:, t, 0], rope[:, t, 1], tm1[:, t])
                    latent_heads_shaped(0)
                    dve.wait_ge(pair_free, q0 + 9)
                    for t in range(TT):
                        m = head_squares(kvc[:, t, 0:256], KV_HEADS, HD, negm[:, 2 * t:2 * t + 2], tm1[:, 0])
                        steps.wait(m)
                    ask_factors(negm[:, 0:4], HD)
                    latent_heads_shaped(1)
                    dve.wait_ge(rstd_ready, n_power[0])
                    for t in range(TT):
                        norm_heads(kvc[:, t, 0:256], KV_HEADS, HD, negm[:, 2 * t:2 * t + 2], hgain[:, 1])
                    AV.done("shaped", dve.memset(st[:, 0, 0], 0.0))
                    AP_.wait(dve, "heads", 0)
                    dve.tensor_copy(qt1[:, 4:8].rearrange("p a b -> p (a b)"), ps[:, 2:4].rearrange("p a b -> p (a b)"))
                    AV.done("heads", dve.tensor_copy(kt1[:, 1], ps[:, 5]))
                    softmax_items(s["n_item"], Items(1), z)
                    copy_output(s["n_tr"] + 2)
                    phase(4, u0 + 8, 2)
                    scale_x(s, (0,))
                    if unscaled(s):
                        dve.sem_inc(ln_used, 1)
                    if unscaled(nxt):
                        factors(nxt)
                    take_y(s, (0,), 4, u0 + 12, True, s["n_tile"])
                elif s["kind"] == "mix":
                    u0, q0, turn = s["n_unit"], s["n_inq"], s["n_mix"]

                    def stage(name, ins_):
                        MV.done(name, ins_)
                        MV.wait(dve, name, turn)
                    def norm_moba(t):
                        for g in range(2):
                            norm_heads(proj[:, t, g * 512:(g + 1) * 512], M_HEADS, M_HD, nrm[:, t, g * 8:(g + 1) * 8],
                                       hgain[:, g, 0:M_HD])

                    def rotate_moba(t):
                        rotate_heads(proj[:, t, 0:1024], 2 * M_HEADS, M_HD, rope2[:, 0, t], rope2[:, 1, t], om[:, t])
                    phase(12, u0, 4, None, nxt)
                    dve.wait_ge(pair_free, q0 + 13)
                    dve.wait_ge(mix_full, 160 * (turn + 1) + 32)
                    MG.wait(dve, "masks", turn)
                    if turn == 0:
                        rope_tables()
                    MA.wait(dve, "cgh", turn)
                    stage("cgl", dve.tensor_tensor(cgl, cg_raw, cgh.bitcast(F32), ALU.subtract))
                    for t in range(TT):
                        m = head_squares(proj[:, t, 0:1024], 2 * M_HEADS, M_HD, nrm[:, t], om[:, t])
                    steps.wait(m)
                    ask_factors(nrm[:], M_HD)
                    steps.link(dve.tensor_scalar(hgain[:, 0, 0:M_HD], hgain[:, 0, 0:M_HD], M_HD ** -0.5, None, ALU.mult))
                    MA.wait(dve, "sig", turn)
                    stage("h", dve.tensor_tensor(hx[:], hx[:], proj[:, :, 1536:1792], ALU.mult))
                    MP.wait(dve, "cg", turn)
                    steps.link(dve.memset(cg_t[:], 1.0))
                    stage("cg_t", dve.tensor_copy(cg_t[0:16], ps[0:16, 6, 0:T]))
                    MP.wait(dve, "z", turn)
                    zg = ps[:, 5].rearrange("p (t c) -> p t c", t=TT)
                    dve.tensor_scalar(e1[:], zg, 0.0, None, ALU.max)
                    steps.link(dve.tensor_scalar(e2[:], zg, 0.0, None, ALU.min))
                    stage("absz", dve.tensor_tensor(e1[:], e2[:], e1[:], ALU.subtract))
                    dve.wait_ge(rstd_ready, n_power[0])
                    norm_moba(0)
                    MA.wait(dve, "softplus", turn)
                    steps.link(dve.tensor_tensor(gg[:], e2[:], e1[:], ALU.subtract))
                    stage("g", dve.tensor_scalar(gg[:], gg[:], 1.0 / 16.0, None, ALU.mult))
                    rotate_moba(0)
                    MA.wait(dve, "decays", turn)
                    c_q, c_k = proj[:, :, 2048:2304], proj[:, :, 2304:2560]
                    dve.scalar_tensor_tensor(out=e1[:], in0=c_q, scalar=G_D ** -0.5, in1=e1[:], op0=ALU.mult, op1=ALU.mult)
                    dve.tensor_tensor(kt[:], c_k, e2[:], ALU.mult)
                    for j in range(2):
                        op = dve.scalar_tensor_tensor(out=ke[:, j], in0=c_k, scalar=tri[:, 64 * j + 63:64 * j + 64],
                                                      in1=e3[:], op0=ALU.mult, op1=ALU.mult)
                    stage("qk", op)
                    norm_moba(1)
                    MP.wait(dve, "qk_t", turn)
                    MA.wait(dve, "qt_t", turn)
                    MG.wait(dve, "zeroed", turn)
                    dve.tensor_copy(kt_t[:].rearrange("p a b -> p (a b)"), ps[0:64, 4:6].rearrange("p a b -> p (a b)"))
                    for h in range(G_HEADS):
                        src = qt_t[:, h].rearrange("p (t j d) -> p t j d", t=TT, j=2)
                        dst = qeo[:, :, h].rearrange("p e (t j d) -> p e t j d", t=TT, j=2)
                        for j in range(2):
                            op = dve.tensor_copy(dst[:, j, :, j], src[:, :, j])
                    stage("kt_t", op)
                    rotate_moba(1)
                    MP.wait(dve, "scores", turn)
                    dve.tensor_tensor(sc_t[:], ps[:, 4:6].rearrange("p a (b c) -> p (a b) c", c=P),
                                      tri.unsqueeze(1).broadcast_to([P, TT * G_HEADS, P]), ALU.mult)
                    steps.link(dve.tensor_copy(kvs[:].rearrange("p a b c -> p (a b c)"),
                                               ps[0:64, 6:8].rearrange("p a b -> p (a b)")))
                    for n in (1, 2):
                        for h in range(G_HEADS):
                            before = kvs[:, h, 0] if n == 1 else sts[:, h, 1]
                            op = dve.scalar_tensor_tensor(out=sts[:, h, n], in0=before, scalar=decay[:, h * 4 + n:h * 4 + n + 1],
                                                          in1=kvs[:, h, n], op0=ALU.mult, op1=ALU.add)
                        steps.link(op)
                    dve.sem_inc(MV.sem, 2)
                    MV.skip("states")
                    MV.skip("shaped")
                    MP.wait(dve, "o", turn)
                    o_c = om[:, :, 768:1024]
                    stage("o_copy", dve.tensor_copy(o_c, ps[:, 0:2, 0:256]))
                    for t in range(TT):
                        m = head_squares(om[:, t, 768:1024], G_HEADS, G_D, nrm_g[:, 4 * t:4 * t + 4], tm2[:, t])
                    steps.wait(m)
                    ask_factors(nrm_g, G_D)
                    MP.wait(dve, "heads", turn)
                    heads_out = dve.tensor_copy(k2[:].rearrange("p a b -> p (a b)"), ps[0:64, 4:8].rearrange("p a b -> p (a b)"))
                    steps.link(heads_out)
                    dve.wait_ge(rstd_ready, n_power[0])
                    for t in range(TT):
                        norm_heads(om[:, t, 768:1024], G_HEADS, G_D, nrm_g[:, 4 * t:4 * t + 4], out_norm)
                    MA.wait(dve, "silu", turn)
                    stage("oc", dve.tensor_tensor(o_c, o_c, gg[:], ALU.mult))
                    dve.sem_inc(MV.sem, 1)
                    MV.skip("k2")
                    MP.wait(dve, "conv", turn)
                    steps.link(dve.tensor_copy(ctok[:].rearrange("p a b -> p (a b)"), ps[:, 6]))
                    grp = ctok[:].rearrange("p t (g c) -> p (t g) c", c=64)
                    for g in range(8):
                        m = steps.mark(dve.bn_stats(hst[:, g], grp[:, g]))
                    steps.wait(m)
                    for g in range(8):
                        m = steps.mark(dve.bn_aggr(hmv[:, g], hst[:, g]))
                    steps.wait(m)
                    steps.link(dve.tensor_scalar(hrs, hmv[:, :, 1], RMS_EPS, None, ALU.add))
                    dve.sem_inc(var_ready, 1)
                    n_power[0] += 1
                    steps.link(dve.tensor_tensor(grp, grp, hmv[:, :, 0:1].broadcast_to([P, 8, 64]), ALU.subtract))
                    dve.wait_ge(rstd_ready, n_power[0])
                    stage("stats", dve.tensor_tensor(grp, grp, hrs.unsqueeze(2).broadcast_to([P, 8, 64]), ALU.mult))
                    for j, op in enumerate((ALU.mult, ALU.add)):
                        last = dve.tensor_tensor(ctok[:], ctok[:], conv_norm[:, j].unsqueeze(1).broadcast_to([P, TT, 256]), op)
                        if j == 0:
                            steps.link(last)
                    stage("o_conv", last)
                    softmax_items(s["n_item"], Items(2), om)
                    copy_output(s["n_tr"] + 1)
                    phase(4, u0 + 12, 2)
                    take_y(s, (0,), 4, u0 + 16, True, s["n_tile"])
                if s["block"] == 1:
                    layer_norm(s)
                else:
                    dve.sem_inc(x_ready, 1)

        @block.tensor
        def _(pe):
            def parts(w_hi, w_lo, x_hi, x_lo):
                return (w_hi, x_hi), (w_lo, x_hi), (w_hi, x_lo)

            def columns(s, sec):
                pe.wait_ge(mod_used, sec * 4 + (12 * s["i"] + 6))
                for c in conds(s):
                    for k in range(KD):
                        m = pe.matmul(ps[:, 4, c * KD + k:c * KD + k + 1], acc[:, c, k * P:(k + 1) * P],
                                      ones[:, 0:1], start=True, stop=True)
                m.then_inc(cols_ready, 1)

            def gate_rows(s):
                pe.wait_ge(mod_used, 12 * s["i"] + 14)
                pe.wait_ge(y_evac, s["n_group"])
                for c in range(len(s["post"])):
                    for half in range(2):
                        m = pe.matmul(ps[:, 4 + 2 * c + half], ones[:], acc[:, c, half * 512:(half + 1) * 512],
                                      start=True, stop=True)
                m.then_inc(gate_ps, 1)

            def transposes(s):
                for k, c in enumerate(s["streams"]):
                    r = s["n_tr"] + k
                    pe.wait_ge(x_ready, s["n_pre"] + k + 1)
                    if s["block"] == 2:
                        pe.wait_ge(z_ready, s["i"] - B2 + 1)
                    pe.wait_ge(tr_act, r)
                    pe.wait_ge(tr_dve, r)
                    src = x[:, c] if s["block"] == 1 else z
                    transpose_stream(src)

            def transpose_stream(src):
                for t in range(TT):
                    for kc in range(KD):
                        off = (kc % 2) * T + t * P
                        m = pe.transpose(ps[:, kc // 2, off:off + P], src[:, t, kc * P:(kc + 1) * P], ident[:])
                m.then_inc(tr_done, 1)

            n_input = [0]

            def features(slot, bank, r, tokens, width):
                for k in range(KD):
                    if k == KD // 2 and r == 0:
                        pe.wait_ge(pre_ready, 2 * n_input[0])
                    at = slice(k * CW + r * P, k * CW + (r + 1) * P)
                    for p, (a, b) in enumerate(parts(wh[:, slot, at], wl[:, slot, at], xh[:, k, tokens], xl[:, k, tokens])):
                        m = pe.matmul(ps[:, bank, 0:width], a, b, start=k == p == 0, stop=k == KD - 1 and p == 2)
                return m

            def features_phase(n, u0, q0, width, per, mods=None):
                def body(idx, j, i):
                    slot, pair = (u0 + j) % 2, (q0 + j) % 2
                    pe.wait_ge(wlo_done, idx + (u0 + 2))
                    pe.wait_ge(pair_free, idx + q0)
                    for r in range(2):
                        m = features(slot, 2 * pair + r, r, slice(0, width), width)
                    m.then_inc(w_used, 1)
                    if mods is not None and section_done(per, j, i) is not None:
                        columns(mods, section_done(per, j, i))
                mod_loop(pe, n, per, body, mods)

            def tokens_phase(n, u0, q0, c, per, mods=None):
                def body(idx, j, i):
                    slot, pair = (u0 + j) % 2, (q0 + j) % 2
                    pe.wait_ge(wlo_done, idx + (u0 + 2))
                    pe.wait_ge(pair_free, idx + q0)
                    for t in range(TT):
                        at = slice(c * T + t * P, c * T + (t + 1) * P)
                        for k in range(KD):
                            if k == KD // 2 and t == 0:
                                pe.wait_ge(pre_ready, 2 * n_input[0])
                            w = slice(k * CW, (k + 1) * CW)
                            for p, (b, a) in enumerate(parts(wh[:, slot, w], wl[:, slot, w], xh[:, k, at], xl[:, k, at])):
                                m = pe.matmul(ps[:, 2 * pair + t, 0:CW], a, b, start=k == p == 0,
                                              stop=k == KD - 1 and p == 2)
                    m.then_inc(w_used, 1)
                    if mods is not None and section_done(per, j, i) is not None:
                        columns(mods, section_done(per, j, i))
                mod_loop(pe, n, per, body, mods)

            def out_unit(u, count, width, bank0, chunk0, ready, start=False, stop=False, halves=None):
                slot = u % 2
                pe.wait_ge(wlo_done, count + 2)
                ready()
                for t in range(width // P):
                    for kk in range(2):
                        at = slice((chunk0 + kk) * width + t * P, (chunk0 + kk) * width + (t + 1) * P)
                        x_hi, x_lo = halves(chunk0 + kk, t) if halves else (hh[:, at], hl[:, at])
                        for half in range(2):
                            w = slice(kk * D + half * 512, kk * D + (half + 1) * 512)
                            for p, (b, a) in enumerate(parts(wh[:, slot, w], wl[:, slot, w], x_hi, x_lo)):
                                m = pe.matmul(ps[:, bank0 + 2 * t + half], a, b, start=start and kk == p == 0,
                                              stop=stop and kk == 1 and p == 2, skip_group_check=not start and not stop)
                    if stop and t < width // P - 1:
                        m.then_inc(y_tile, 1)
                m.then_inc(w_used, 1)

            def add_zero(banks, start):
                for b in banks:
                    for at in range(0, 512, P):
                        m = pe.matmul(ps[:, b, at:at + P], zeros[:], zeros[:], start=start and at == 0, stop=not start,
                                      skip_group_check=True)
                return m

            def out_phase(n, u0, width, bank0, ready, halves=None):
                for i in range(n):
                    out_unit(u0 + i, u0 + i, width, bank0, 2 * i, lambda: ready(i), i == 0, i == n - 1, halves)

            def input_halves(chunk, t):
                return tuple(w[:, chunk, t * P:(t + 1) * P] for w in (xh, xl))

            def attention(n0, items, q, k, v):
                def scores(n):
                    h, t, keys = items[n]
                    if n >= 2:
                        pe.wait_ge(p_ready, n0 + n - 1)
                    m = pe.matmul(ps[:, n % 2, 0:keys], q[:, h, t * P:(t + 1) * P], k(h)[:, 0:keys], start=True,
                                  stop=not items.masked)
                    if items.masked:
                        m = pe.matmul(ps[:, n % 2, keys - P:keys], ident[:], causal, start=False, stop=True)
                    m.then_inc(s_ps, 1)

                for n in range(2):
                    scores(n)
                for n, (h, t, keys) in enumerate(items):
                    pe.wait_ge(p_ready, n0 + n + 1)
                    if n >= 2:
                        pe.wait_ge(pt_ready, n0 + n - 1)
                    for a in range(0, keys, P):
                        m = pe.transpose(ps[:, 2 + n % 2, a:a + P], sg[:, n % 2, a:a + P], ident[:])
                    m.then_inc(pt_ps, 1)
                    if n + 2 < len(items):
                        scores(n + 2)
                    pe.wait_ge(pt_ready, n0 + n + 1)
                    if n >= 2:
                        pe.wait_ge(o_taken, n0 + n - 1)
                    for c in range(keys // P):
                        m = pe.matmul(ps[:, 4 + n % 2, 0:items.d], ht[:, n % 2, c * P:(c + 1) * P], v(h, c),
                                      start=c == 0, stop=c == keys // P - 1)
                    m.then_inc(o_ps, 1)

            pe.wait_ge(ident_ready, 2)
            pe.wait_ge(ws_full, 16)
            for g in range(SG_GROUPS):
                m = pe.transpose(ps[:, g // 4, (g % 4) * P:(g % 4 + 1) * P],
                                 ht[:, g // 4, (g % 4) * P:(g % 4 + 1) * P], ident[:])
                if g % 4 == 3:
                    m.then_inc(wst_ps, 1)
            pe.wait_ge(svec_ready, 1)
            cs = slice(2, 3) if subs[0]["block"] == 2 else slice(0, 2)
            nc_ = len(conds(subs[0]))
            for n in range(8):
                sec, q = divmod(n, 4)
                pe.wait_ge(first_full[n % 6], 16 * (n // 6 + 1))
                for half in range(2):
                    for jj in range(2):
                        m = pe.matmul(ps[0:nc_, 4 + 2 * sec + half], svec[:, cs, 2 * q + jj],
                                      first_w[:, n % 6, jj, half * 512:(half + 1) * 512],
                                      start=q == jj == 0, stop=q == 3 and jj == 1)
                m.then_inc(first_used, 1)
            for sec in range(2):
                pe.wait_ge(first_rows, sec + 1)
                for kc in range(KD):
                    m = pe.transpose(ps[:, 2 + sec, nc_ * kc:nc_ * (kc + 1)], gate[0:nc_, sec, kc * P:(kc + 1) * P],
                                     ident[0:nc_, 0:nc_])
                m.then_inc(cols_ready, 1)
            pe.wait_ge(mcol_done, 2)
            pe.wait_ge(wst_ready, 2)
            for s in subs:
                nxt = after(s)
                gate_rows(s)
                transposes(s)
                n_input[0] = s["n_tr"] + len(s["streams"])
                pe.wait_ge(pre_ready, 2 * n_input[0] - 1)
                if s["kind"] == "ffn":
                    W = T * len(s["streams"])
                    both = W == 2 * T
                    m0, u0 = 0, s["n_unit"]
                    for g, n in enumerate(GROUPS):
                        if both:
                            pe.wait_ge(y_evac, s["n_group"] + g)
                        features_phase(n, u0, s["n_inq"] + m0, W, 2 if g else 4, None if g else nxt)
                        pe.wait_ge(pair_free, s["n_inq"] + m0 + n + 1)
                        pe.wait_ge(y_evac, s["n_group"] + g)
                        if g == 0 and nxt:
                            pe.wait_ge(mcol_done, 2 * s["i"] + 4)
                        out_phase(n // 2, u0 + n, W, 0 if both else 4,
                                  lambda i: pe.wait_ge(h_ready, s["n_h"] + m0 + 2 * i + 3))
                        m0 += n
                        u0 += n + n // 2
                elif s["kind"] == "gmlp":
                    for k, c in enumerate(s["streams"]):
                        u0, q0 = s["n_unit"] + 36 * k, s["n_inq"] + 24 * k
                        tokens_phase(12, u0, q0, c, 4, nxt if k == 0 else None)
                        u1, q1, h1 = u0 + 12, q0 + 12, s["n_h"] + 12 * k
                        pe.wait_ge(y_evac, s["n_group"] + k)
                        pe.wait_ge(bs_full, 16)
                        if k == 0 and nxt:
                            pe.wait_ge(mcol_done, 2 * s["i"] + 4)
                        add_zero(range(4, 8), True)

                        def group(idx, j, i):
                            for q in range(3):
                                slot, pair = (u1 + q) % 2, q % 2
                                pe.wait_ge(wlo_done, idx * 6 + (u1 + q + 2))
                                pe.wait_ge(pair_free, idx * 3 + (q1 + q + (1 if q == 0 else 0)))
                                if q == 0:
                                    pe.wait_ge(vg_ready, idx + (GM_STEPS * k + 1))
                                for r in range(2):
                                    features(slot, 2 * pair + r, r, slice(c * T, (c + 1) * T), T)
                                for r in range(2):
                                    m = 2 * q + r
                                    g = idx * 2 + m // 3
                                    for t in range(TT):
                                        to = ps[:, 2 * pair + r, T + t * P:T + (t + 1) * P]
                                        pe.matmul(to, vg[:, t, m * P:(m + 1) * P],
                                                  wst[:, bass.ds(g, 1), :].rearrange("p a b -> p (a b)"),
                                                  start=True, stop=False)
                                        last = pe.matmul(to, ones[0:1, :], bsrow[:, bass.ds(g * P, P)],
                                                         start=False, stop=True)
                                last.then_inc(w_used, 1)
                            for q in range(3):
                                out_unit(u1 + 3 + q, idx * 6 + (u1 + 3 + q), T, 4, 2 * q,
                                         lambda: pe.wait_ge(h_ready, idx * 3 + (h1 + q + 2)))
                        loop(pe, GM_STEPS, 1, group)
                        add_zero(range(4, 8), False).then_inc(y_closed, 1)
                elif s["kind"] == "attn":
                    u0, q0 = s["n_unit"], s["n_inq"]
                    tokens_phase(6, u0, q0, 0, 6, nxt)
                    tokens_phase(2, u0 + 6, q0 + 6, 1, 2)
                    AV.wait(pe, "shaped", 0)
                    pe.wait_ge(pair_free, q0 + 9)
                    for n in range(HEADS * TT):
                        h, t = divmod(n, TT)
                        pe.transpose(ps[:, n // 4, (n % 4) * P:(n % 4 + 1) * P], ql[:, t, h * HD:(h + 1) * HD], ident[:])
                    for h in range(KV_HEADS):
                        for t in range(2 * TT):
                            src = kvc[:, t] if t < TT else ql[:, t - TT, HEADS * HD:]
                            m = pe.transpose(ps[:, 4 + h, t * P:(t + 1) * P], src[:, h * HD:(h + 1) * HD], ident[:])
                    AP_.done("heads", m)
                    AA.wait(pe, "heads", 0)
                    AV.wait(pe, "heads", 0)

                    def values(h, c):
                        at = (h // (HEADS // KV_HEADS) + KV_HEADS) * HD
                        src = kvc[:, c] if c < TT else ql[:, c - TT, HEADS * HD:]
                        return src[:, at:at + HD]
                    items = Items(1)
                    attention(s["n_item"], items, qt1, lambda h: kt1[:, h // (HEADS // KV_HEADS)], values)
                    pe.wait_ge(o_taken, s["n_item"] + len(items))
                    transpose_stream(z)
                    pe.wait_ge(pre_ready, 2 * (s["n_tr"] + 3))
                    out_phase(4, u0 + 8, T, 4, lambda i: None, input_halves)
                elif s["kind"] == "mix":
                    u0, q0, turn = s["n_unit"], s["n_inq"], s["n_mix"]
                    tokens_phase(12, u0, q0, 0, 4, nxt)
                    MV.wait(pe, "cgl", turn)
                    for k in range(KD):
                        w = slice(k * 16, (k + 1) * 16)
                        for p, (a, b) in enumerate(parts(cgh[:, w], cgl[:, w], xh[:, k, 0:T], xl[:, k, 0:T])):
                            m = pe.matmul(ps[0:16, 6, 0:T], a, b, start=k == p == 0, stop=k == KD - 1 and p == 2)
                    MP.done("cg", m)
                    MV.wait(pe, "h", turn)
                    for cc in range(2):
                        for t in range(TT):
                            pe.transpose(ps[:, 2, cc * T + t * P:cc * T + (t + 1) * P], hx[:, t, cc * P:(cc + 1) * P], ident[:])
                        m = pe.transpose(ps[:, 1, cc * 32:(cc + 1) * 32], conv_raw[:, cc * P:(cc + 1) * P], ident[0:32, 0:32])
                    MP.done("h_t", m)

                    def taps(start, end):
                        if start == 0:
                            MA.wait(pe, "ch_t", turn)
                            MG.wait(pe, "zeroed", turn)
                        for n in range(start, end):
                            cc, tap = divmod(n, CONV_K)
                            pe.wait_ge(tap_ready, 2 * CONV_K * turn + n + 1)
                            m = pe.matmul(ps[:, 3, cc * T:(cc + 1) * T], sg[:, n % 8 // 4, n % 4 * P:(n % 4 + 1) * P],
                                          ch_t[:, cc, tap:tap + T], start=tap == 0, stop=tap == CONV_K - 1)
                            m.then_inc(tap_used, 1)
                    MV.wait(pe, "cg_t", turn)
                    for t in range(TT):
                        m = pe.matmul(ps[:, 5, t * T:(t + 1) * T], cg_t[0:17, t * P:(t + 1) * P], gate_raw[0:17],
                                      start=True, stop=True)
                    MP.done("z", m)
                    taps(0, 8)
                    MV.wait(pe, "g", turn)
                    for t in range(TT):
                        for bank, mask in ((5, tri), (6, suf)):
                            pe.matmul(ps[:, bank, t * T:(t + 1) * T], mask, gg[:, t], start=True, stop=True)
                        for h in range(G_HEADS):
                            at = (h * TT + t) * 2
                            m = pe.matmul(ps[0:64, 7, at:at + 2], gg[:, t, h * G_D:(h + 1) * G_D], tri[:, 63:P:64],
                                          start=True, stop=True)
                    MP.done("sums", m)
                    taps(8, 24)
                    MV.wait(pe, "qk", turn)
                    for bank, src in ((0, e1), (4, kt)):
                        for h in range(G_HEADS):
                            for t in range(TT):
                                at = (h % 2) * T + t * P
                                m = pe.transpose(ps[0:64, bank + h // 2, at:at + P], src[:, t, h * G_D:(h + 1) * G_D], ident[:])
                    MP.done("qk_t", m)
                    MA.wait(pe, "qt_t", turn)
                    MV.wait(pe, "kt_t", turn)
                    for t in range(TT):
                        for h in range(G_HEADS):
                            pe.matmul(ps[:, 4 + t, h * P:(h + 1) * P], kt_t[:, h, t * P:(t + 1) * P],
                                      qt_t[:, h, t * P:(t + 1) * P], start=True, stop=True)
                            cv = proj[:, t, 2560 + h * G_D:2560 + (h + 1) * G_D]
                            for j in range(2):
                                at = (h % 2) * T + (2 * t + j) * G_D
                                m = pe.matmul(ps[0:64, 6 + h // 2, at:at + G_D], ke[:, j, t, h * G_D:(h + 1) * G_D], cv,
                                              start=True, stop=True)
                    MP.done("scores", m)
                    taps(24, 40)
                    MV.wait(pe, "states", turn)
                    for t in range(TT):
                        for h in range(G_HEADS):
                            to = ps[:, t, h * G_D:(h + 1) * G_D]
                            pe.matmul(to, sc_t[:, t * G_HEADS + h], proj[:, t, 2560 + h * G_D:2560 + (h + 1) * G_D],
                                      start=True, stop=False)
                            for j in range(0 if t else 1, 2):
                                n = 2 * t + j
                                state = kvs[:, h, 0] if n == 1 else sts[:, h, n - 1]
                                m = pe.matmul(to, qeo[:, j, h, t * P:(t + 1) * P], state, start=False, stop=j == 1)
                    MP.done("o", m)
                    taps(40, 2 * CONV_K)
                    pe.wait_ge(tap_used, 2 * CONV_K * (turn + 1))
                    pe.sem_inc(MP.sem, 1)
                    MP.skip("taps")
                    MA.wait(pe, "cacc", turn)
                    MV.wait(pe, "o_copy", turn)
                    MV.wait(pe, "shaped", turn)
                    for g in range(2):
                        for h in range(M_HEADS):
                            for t in range(TT):
                                at = (h % 2) * T + t * P
                                src = proj[:, t, g * 512 + h * M_HD:g * 512 + (h + 1) * M_HD]
                                m = pe.transpose(ps[0:64, 4 * g + h // 2, at:at + P], src, ident[:])
                    MP.done("heads", m)
                    MV.wait(pe, "k2", turn)
                    MA.wait(pe, "q2", turn)
                    for cc in range(2):
                        for t in range(TT):
                            m = pe.transpose(ps[:, 6, t * T + cc * P:t * T + (cc + 1) * P], cacc[:, cc, t * P:(t + 1) * P], ident[:])
                    MP.done("conv", m)
                    items = Items(2)
                    attention(s["n_item"], items, q2, lambda h: k2[:, h],
                              lambda h, c: proj[:, c, 1024 + h * M_HD:1024 + (h + 1) * M_HD])
                    pe.wait_ge(o_taken, s["n_item"] + len(items))
                    MA.wait(pe, "conv", turn)
                    transpose_stream(om)
                    pe.wait_ge(pre_ready, 2 * (s["n_tr"] + 2))
                    out_phase(4, u0 + 12, T, 4, lambda i: None, input_halves)


_INS = ("x", "c", "ctx", "c_ctx", "w_mod", "b_mod", "ln_g", "ln_b", "ffn_w_in", "ffn_w_out", "gmlp_w_in", "gmlp_ln_g",
        "gmlp_ln_b", "gmlp_w_s", "gmlp_b_s", "gmlp_w_out", "attn_w_qkv", "attn_q_norm", "attn_k_norm", "attn_w_o",
        "c_2", "positions_2", "ada_w_2", "ada_b_2", "ffn1_norm_2", "ffn1_w_in_2", "ffn1_w_out_2", "mix_norm_2",
        "mix_w_in_2", "q_norm_2", "k_norm_2", "conv_w_2", "conv_b_2", "conv_norm_g_2", "conv_norm_b_2",
        "gla_gate_w_2", "gla_gate_b_2", "gla_out_norm_2", "mix_w_out_2", "ffn2_norm_2", "ffn2_w_in_2", "ffn2_w_out_2")


def rope_constants():
    quarter = HD // 4
    freqs = (10000.0 ** (-np.arange(quarter) / quarter)).astype(np.float32)
    t = np.arange(T)
    ang = np.concatenate([(t // 64).astype(np.float32)[:, None] * freqs, (t % 64).astype(np.float32)[:, None] * freqs], -1)
    inv = np.float32(1.0) / (10000.0 ** (np.arange(0, M_HD, 2) / M_HD)).astype(np.float32)
    return (np.stack([np.cos(ang), np.sin(ang)]).astype(np.float32), inv.astype(np.float32)[None])


def kernel(**inputs):
    import concourse.bacc as bacc
    from concourse.bass_utils import run_bass_kernel_spmd

    nc = bacc.Bacc("TRN2", target_bir_lowering=False, num_devices=1)
    arrays = {n: np.ascontiguousarray(inputs[n]) for n in _INS}
    arrays["rope_1"], arrays["rope_freqs_2"] = rope_constants()
    ins = {n: nc.dram_tensor(f"in_{n}", a.shape, mybir.dt.from_np(a.dtype), kind="ExternalInput").ap()
           for n, a in arrays.items()}
    out = nc.dram_tensor("out_0", (1, T, D), F32, kind="ExternalOutput").ap()
    program(nc, ins, out, plan())
    r = run_bass_kernel_spmd(nc, [{f"in_{n}": a for n, a in arrays.items()}], core_ids=[0])
    return r.results[0]["out_0"]
```
